# Optimizing a Trainium2 kernel written in Bass

```python
import jax
import jax.numpy as jnp
from jax import lax
import numpy as np

D_MODEL = 1024
BATCH = 1
SEQ = 1024
DEPTH = 1

CHUNK = 64
A_HEADS = 8
A_HEAD_DIM = 64
KV_RANK = 128
IDX_HEADS = 8
IDX_DIM = 64
MAX_SELECTED = 256
M_HEADS = 4
M_HEAD_DIM = 128
CONV_WIDTH = 4
N_EXPERTS = 32
TOP_EXPERTS = 4
D_EXPERT = D_MODEL
SWIGLU_LIMIT = 7.0
SWIGLU_ALPHA = 1.702
EXPERT_BLOCK = 128
LN_EPS = 1e-5
DN_ALPHA = (2.0 * DEPTH) ** 0.25
DN_BETA = (8.0 * DEPTH) ** -0.25

A_WIDTH = A_HEADS * A_HEAD_DIM
M_WIDTH = M_HEADS * M_HEAD_DIM
MIX_WIDTH = A_WIDTH + M_WIDTH
IN_SIZES = (A_WIDTH, KV_RANK, IDX_HEADS * IDX_DIM, IDX_DIM, IDX_HEADS,
            M_WIDTH, M_WIDTH, M_WIDTH, M_HEADS, M_HEADS)
IN_WIDTH = sum(IN_SIZES)
IN_SPLITS = tuple(int(v) for v in np.cumsum(IN_SIZES)[:-1])

kernel_name = "hybrid_dsa_mlstm_moe_deepnorm"

def layer_norm(x, g, b):
    xf = x.astype(jnp.float32)
    mu = xf.mean(-1, keepdims=True)
    var = jnp.square(xf - mu).mean(-1, keepdims=True)
    return ((xf - mu) * lax.rsqrt(var + LN_EPS) * g + b).astype(x.dtype)

def rms_norm(x, g):
    xf = x.astype(jnp.float32)
    ms = jnp.square(xf).mean(-1, keepdims=True)
    return (xf * lax.rsqrt(ms + LN_EPS) * g).astype(x.dtype)

def alibi_slopes(n):
    return jnp.asarray(2.0 ** (-8.0 * np.arange(1, n + 1) / n), dtype=jnp.float32)

def to_chunks(t, nc):
    return jnp.moveaxis(t.reshape(t.shape[0], nc, CHUNK, *t.shape[2:]), 1, 0)

def dsa_attention(q, c_kv, q_idx, k_idx, w_idx, kv_norm_g, w_uk, w_uv):
    B, S = q.shape[:2]
    nc = S // CHUNK
    k_sel = min(MAX_SELECTED, S // 4)
    c = rms_norm(c_kv, kv_norm_g)
    q_lat = jnp.einsum('bshd,hrd->bshr', q, w_uk) * (A_HEAD_DIM ** -0.5)
    slopes = alibi_slopes(A_HEADS)
    key_chunk = jnp.arange(S) // CHUNK

    def chunk_block(args):
        ci, q_b, qi_b, wi_b = args
        qpos = ci * CHUNK + jnp.arange(CHUNK)
        rel = jax.nn.relu(jnp.einsum('bthd,bsd->bths', qi_b, k_idx))
        score = jnp.einsum('bths,bth->bts', rel, wi_b)
        score = jnp.where((key_chunk <= ci)[None, None, :], score, -jnp.inf)
        top_s, top_i = lax.top_k(score, k_sel)
        valid = jnp.isfinite(top_s)
        c_sel = jax.vmap(lambda cb, ib: cb[ib])(c, top_i)
        logits = jnp.einsum('bthr,btkr->bthk', q_b, c_sel).astype(jnp.float32)
        dist = jnp.abs(qpos[None, :, None] - top_i).astype(jnp.float32)
        logits = logits - slopes[None, None, :, None] * dist[:, :, None, :]
        logits = jnp.where(valid[:, :, None, :], logits, -jnp.inf)
        p = jax.nn.softmax(logits, axis=-1).astype(c_sel.dtype)
        return jnp.einsum('bthk,btkr->bthr', p, c_sel)

    xs = (jnp.arange(nc), to_chunks(q_lat, nc), to_chunks(q_idx, nc), to_chunks(w_idx, nc))
    o_lat = lax.map(chunk_block, xs)
    o_lat = jnp.moveaxis(o_lat, 0, 1).reshape(B, S, A_HEADS, KV_RANK)
    o = jnp.einsum('bshr,hrd->bshd', o_lat, w_uv)
    return o.reshape(B, S, A_WIDTH)

def causal_conv(u, w, b):
    y = lax.conv_general_dilated(u, w[:, None, :], window_strides=(1,),
                                 padding=[(CONV_WIDTH - 1, 0)],
                                 dimension_numbers=('NWC', 'WIO', 'NWC'),
                                 feature_group_count=u.shape[-1])
    return y + b

def mlstm(u, v, z, i_pre, f_pre, conv_w, conv_b, w_mq, w_mk, norm_g):
    B, S, _ = u.shape
    nc = S // CHUNK
    f32 = jnp.float32
    uc = jax.nn.silu(causal_conv(u, conv_w, conv_b)).reshape(B, S, M_HEADS, M_HEAD_DIM)
    q = jnp.einsum('bshd,hde->bhse', uc, w_mq).astype(f32)
    k = (jnp.einsum('bshd,hde->bhse', uc, w_mk) * (M_HEAD_DIM ** -0.5)).astype(f32)
    vh = v.reshape(B, S, M_HEADS, M_HEAD_DIM).transpose(0, 2, 1, 3).astype(f32)
    chunked = lambda t: t.reshape(B, M_HEADS, nc, CHUNK, *t.shape[3:])
    qc, kc, vc = chunked(q), chunked(k), chunked(vh)
    li = chunked(i_pre.astype(f32).transpose(0, 2, 1))
    lf = chunked(jax.nn.log_sigmoid(f_pre.astype(f32)).transpose(0, 2, 1))
    b = jnp.cumsum(lf, axis=-1)
    b_tot = b[..., -1]
    a = b_tot[..., None] - b + li
    a_max = a.max(-1)

    def step(carry, inp):
        C, n, m = carry
        kk, vv, aa, amax, btot = inp
        m_new = jnp.maximum(btot + m, amax)
        decay = jnp.exp(btot + m - m_new)
        w = jnp.exp(aa - m_new[..., None])
        C_new = decay[..., None, None] * C + jnp.einsum('bhl,bhlv,bhlk->bhvk', w, vv, kk)
        n_new = decay[..., None] * n + jnp.einsum('bhl,bhlk->bhk', w, kk)
        return (C_new, n_new, m_new), (C, n, m)

    init = (jnp.zeros((B, M_HEADS, M_HEAD_DIM, M_HEAD_DIM), f32),
            jnp.zeros((B, M_HEADS, M_HEAD_DIM), f32),
            jnp.full((B, M_HEADS), -1e30, f32))
    mv = lambda t: jnp.moveaxis(t, 2, 0)
    _, (C_prev, n_prev, m_prev) = lax.scan(step, init, (mv(kc), mv(vc), mv(a), mv(a_max), mv(b_tot)))
    C_prev = jnp.moveaxis(C_prev, 0, 2)
    n_prev = jnp.moveaxis(n_prev, 0, 2)
    m_prev = jnp.moveaxis(m_prev, 0, 2)

    g = b + m_prev[..., None]
    causal = jnp.tril(jnp.ones((CHUNK, CHUNK), bool))
    dlog = jnp.where(causal, b[..., :, None] - b[..., None, :] + li[..., None, :], -jnp.inf)
    m_t = jnp.maximum(g, dlog.max(-1))
    w_intra = jnp.exp(dlog - m_t[..., None])
    w_state = jnp.exp(g - m_t)
    s = jnp.einsum('bhcte,bhcse->bhcts', qc, kc) * w_intra
    num = (jnp.einsum('bhcts,bhcsv->bhctv', s, vc)
           + w_state[..., None] * jnp.einsum('bhcvk,bhctk->bhctv', C_prev, qc))
    den = s.sum(-1) + w_state * jnp.einsum('bhck,bhctk->bhct', n_prev, qc)
    hc = num / jnp.maximum(jnp.abs(den), jnp.exp(-m_t))[..., None]
    hc = hc.reshape(B, M_HEADS, S, M_HEAD_DIM)
    mu = hc.mean(-1, keepdims=True)
    var = jnp.square(hc - mu).mean(-1, keepdims=True)
    hc = (hc - mu) * lax.rsqrt(var + LN_EPS)
    h = hc.transpose(0, 2, 1, 3).reshape(B, S, M_WIDTH) * norm_g
    return (jax.nn.sigmoid(z.astype(f32)) * h).astype(u.dtype)

def moe(x, w_router, b_router, w_gu, b_gu, w_down, b_down):
    B, S, D = x.shape
    T = B * S
    xf = x.reshape(T, D)
    logits = (xf @ w_router + b_router).astype(jnp.float32)
    top_v, top_e = lax.top_k(logits, TOP_EXPERTS)
    gates = jax.nn.softmax(top_v, axis=-1)
    A = T * TOP_EXPERTS
    flat_e = top_e.reshape(A)
    flat_tok = jnp.arange(A, dtype=jnp.int32) // TOP_EXPERTS
    flat_g = gates.reshape(A)
    order = jnp.argsort(flat_e)
    se = flat_e[order]
    counts = jnp.bincount(flat_e, length=N_EXPERTS)
    padded = (counts + EXPERT_BLOCK - 1) // EXPERT_BLOCK * EXPERT_BLOCK
    start = jnp.cumsum(counts) - counts
    pad_end = jnp.cumsum(padded)
    pad_start = pad_end - padded
    dest = pad_start[se] + jnp.arange(A, dtype=jnp.int32) - start[se]
    P = A + N_EXPERTS * EXPERT_BLOCK
    nb = P // EXPERT_BLOCK
    row_tok = jnp.zeros((P,), jnp.int32).at[dest].set(flat_tok[order])
    row_gate = jnp.zeros((P,), jnp.float32).at[dest].set(flat_g[order])
    blk_e = jnp.minimum(jnp.searchsorted(pad_end, jnp.arange(nb) * EXPERT_BLOCK, side='right'),
                        N_EXPERTS - 1)

    def expert_block(args):
        e, tok, gt = args
        xb = xf[tok]
        gu = xb @ w_gu[e] + b_gu[e]
        gate, up = gu[:, :D_EXPERT], gu[:, D_EXPERT:]
        gate = jnp.minimum(gate, SWIGLU_LIMIT)
        up = jnp.clip(up, -SWIGLU_LIMIT, SWIGLU_LIMIT)
        h = (up + 1.0) * gate * jax.nn.sigmoid(SWIGLU_ALPHA * gate)
        y = h @ w_down[e] + b_down[e]
        return y * gt[:, None].astype(y.dtype)

    ys = lax.map(expert_block, (blk_e, row_tok.reshape(nb, EXPERT_BLOCK),
                                row_gate.reshape(nb, EXPERT_BLOCK)))
    y = jax.ops.segment_sum(ys.reshape(P, D), row_tok, num_segments=T)
    return y.reshape(B, S, D).astype(x.dtype)

def setup_inputs(seed: int = 0) -> dict:
    key = jax.random.key(seed)
    ks = jax.random.split(key, 24)
    nrm = lambda k, shape, scale: jax.random.normal(k, shape, jnp.float32) * scale
    L = DEPTH
    return {
        "x": nrm(ks[0], (BATCH, SEQ, D_MODEL), 1.0),
        "w_in": nrm(ks[1], (L, D_MODEL, IN_WIDTH), D_MODEL ** -0.5),
        "kv_norm_g": 1.0 + nrm(ks[2], (L, KV_RANK), 0.05),
        "w_uk": nrm(ks[3], (L, A_HEADS, KV_RANK, A_HEAD_DIM), KV_RANK ** -0.5),
        "w_uv": nrm(ks[4], (L, A_HEADS, KV_RANK, A_HEAD_DIM), KV_RANK ** -0.5),
        "m_conv_w": nrm(ks[5], (L, CONV_WIDTH, M_WIDTH), CONV_WIDTH ** -0.5),
        "m_conv_b": nrm(ks[6], (L, M_WIDTH), 0.01),
        "w_mq": nrm(ks[7], (L, M_HEADS, M_HEAD_DIM, M_HEAD_DIM), M_HEAD_DIM ** -0.5),
        "w_mk": nrm(ks[8], (L, M_HEADS, M_HEAD_DIM, M_HEAD_DIM), M_HEAD_DIM ** -0.5),
        "b_i": nrm(ks[9], (L, M_HEADS), 0.1),
        "b_f": jnp.linspace(3.0, 6.0, M_HEADS)[None, :] + nrm(ks[10], (L, M_HEADS), 0.1),
        "m_norm_g": 1.0 + nrm(ks[11], (L, M_WIDTH), 0.05),
        "w_out": nrm(ks[12], (L, MIX_WIDTH, D_MODEL), DN_BETA * MIX_WIDTH ** -0.5),
        "ln1_g": 1.0 + nrm(ks[13], (L, D_MODEL), 0.05),
        "ln1_b": nrm(ks[14], (L, D_MODEL), 0.01),
        "w_router": nrm(ks[15], (L, D_MODEL, N_EXPERTS), D_MODEL ** -0.5),
        "b_router": nrm(ks[16], (L, N_EXPERTS), 0.01),
        "w_gu": nrm(ks[17], (L, N_EXPERTS, D_MODEL, 2 * D_EXPERT), D_MODEL ** -0.5),
        "b_gu": nrm(ks[18], (L, N_EXPERTS, 2 * D_EXPERT), 0.01),
        "w_down": nrm(ks[19], (L, N_EXPERTS, D_EXPERT, D_MODEL), DN_BETA * D_EXPERT ** -0.5),
        "b_down": nrm(ks[20], (L, N_EXPERTS, D_MODEL), 0.01),
        "ln2_g": 1.0 + nrm(ks[21], (L, D_MODEL), 0.05),
        "ln2_b": nrm(ks[22], (L, D_MODEL), 0.01),
    }

def reference(x, w_in, kv_norm_g, w_uk, w_uv, m_conv_w, m_conv_b, w_mq, w_mk, b_i, b_f,
              m_norm_g, w_out, ln1_g, ln1_b, w_router, b_router, w_gu, b_gu, w_down, b_down,
              ln2_g, ln2_b):
    B, S, _ = x.shape
    h = x
    for l in range(DEPTH):
        proj = h @ w_in[l]
        q_a, ckv, q_i, k_i, w_i, u, v, z, i_pre, f_pre = jnp.split(proj, IN_SPLITS, axis=-1)
        a_out = dsa_attention(q_a.reshape(B, S, A_HEADS, A_HEAD_DIM), ckv,
                              q_i.reshape(B, S, IDX_HEADS, IDX_DIM), k_i, w_i,
                              kv_norm_g[l], w_uk[l], w_uv[l])
        m_out = mlstm(u, v, z, i_pre + b_i[l], f_pre + b_f[l], m_conv_w[l], m_conv_b[l],
                      w_mq[l], w_mk[l], m_norm_g[l])
        mix = jnp.concatenate([a_out, m_out], axis=-1) @ w_out[l]
        h = layer_norm(DN_ALPHA * h + mix, ln1_g[l], ln1_b[l])
        ffn = moe(h, w_router[l], b_router[l], w_gu[l], b_gu[l], w_down[l], b_down[l])
        h = layer_norm(DN_ALPHA * h + ffn, ln2_g[l], ln2_b[l])
    return h


_drawn_inputs = setup_inputs


def setup_inputs(seed=0):
    import zlib

    import numpy as np

    out = dict(_drawn_inputs(seed))
    spreads = {}
    factors = {'kv_norm_g': 3.368,
     'm_conv_b': 5.045,
     'b_i': 64.0,
     'm_norm_g': 3.021,
     'ln1_b': 2.935,
     'b_router': 3.183,
     'b_gu': 8.0,
     'b_down': 8.0,
     'ln2_b': 5.669}
    for name, (base, spread) in spreads.items():
        noise = np.random.default_rng([zlib.crc32(name.encode()), seed]).standard_normal(out[name].shape)
        drawn = base * np.exp(spread * noise) if base else spread * noise
        out[name] = jnp.asarray(drawn.astype(out[name].dtype))
    for name, factor in factors.items():
        out[name] = (out[name] * factor).astype(out[name].dtype)
    return out
```

```python
from contextlib import ExitStack

import concourse.bass as bass
from concourse import mybir

P = 128
D = 1024
S = 1024
NT = S // P
KT = D // P
SLAB = 512
AH, AD = 8, 64
R = 128
MH, MD = 4, 128
SMALL = R + 8 + 4 + 4
NE = 32
CAP = 2 * P
MAX_ITEMS = 64
TOPK = 256
PICKED = -1e30
OUTSIDE = -2e30
FAR = 1e30
EPS = 1e-5
ALPHA = 2.0 ** 0.25
LIMIT = 7.0
HROW = D + NE

C_ID, C_MASK, C_DIST, C_IOTA, C_QS, C_BASE, C_COL, C_ONE, C_END = (
    0, 128, 256, 1280, 1536, 1540, 1606, 1608, 1736)


def chunks(t):
    n = P * (t + 1)
    return [(a, min(a + SLAB, n)) for a in range(0, n, SLAB)]


def groups(t):
    return [(a, min(a + 4, t + 1)) for a in range(0, t + 1, 4)]


def task_order():
    o = [("qi", m, n) for n in range(2) for m in range(4)] + [("ki", n) for n in range(2)]
    o += [("small", j) for j in range(4)]
    o += [("sc", t, h, c) for t in range(2, NT) for h in range(AH) for c in range(len(chunks(t)))]
    o += [("grow",)]
    o += [("qa", m, n) for n in range(2) for m in range(4)]
    o += [("grow2",), ("mprev",)]
    o += [("u", m, n) for n in range(2) for m in range(4)]
    o += [("gcol",)]
    o += [("v", t) for t in range(NT)] + [("z", t) for t in range(NT)]
    o += [("ct", j) for j in range(2)]
    for c in range(NT):
        o += [("mq", c), ("mk", c), ("mkt", c), ("R", c), ("S", c)]
        o += [("X", c, q) for q in range(2) if c]
        o += [("I", c, q) for q in range(2)]
        o += [("U", c, q) for q in range(2) if c < NT - 1]
    o += [("mt", c) for c in range(NT)]
    o += [("kt", m, n) for n in range(2) for m in range(4)] + [("V", t) for t in range(NT)]
    for n in range(NT * AH + 4):
        if n < NT * AH:
            o += [("L", n, c) for c in range(len(chunks(n // AH)))]
        if 1 <= n <= NT * AH:
            o += [("T", n - 1, g) for g in range(len(groups((n - 1) // AH)))]
        if n >= 11 and n % AH == 3:
            o += [("at", n // AH - 1)]
    for t in range(NT):
        o += [("mix", t, 0), ("mix", t, 1)]
        if t:
            o += [("ht", t - 1, 0), ("ht", t - 1, 1)]
        if t > 1:
            o += [("rt", t - 2), ("rtt", t - 2)]
    o += [("ht", NT - 1, 0), ("ht", NT - 1, 1)]
    for t in (NT - 2, NT - 1):
        o += [("rt", t), ("rtt", t)]
    o += [("cnt",), ("items",)] + [("gt", j) for j in range(2)]
    o += [("bd", t, n) for t in range(NT) for n in range(2)]
    return o


NB = 7
ORDER = task_order()
PLACE = {task: (n % NB, n // NB) for n, task in enumerate(ORDER)}


def layer_kernel(nc, a, out):
    f32, f32r, bf16 = mybir.dt.float32, mybir.dt.float32r, mybir.dt.bfloat16
    i32, u32 = mybir.dt.int32, mybir.dt.uint32
    ALU, ACT, AX = mybir.AluOpType, mybir.ActivationFunctionType, mybir.AxisListType

    ctx = ExitStack()
    with ctx:
        KB = 1024
        LOW = 16512

        def at(name, kb, shape, dt=f32):
            return nc.alloc_sbuf_tensor_at(name, shape, dt, offset=LOW + int(kb * KB) // 32 * 32)

        def sem(name):
            return ctx.enter_context(nc.semaphore(name))

        raw = at("raw", 0, [P, 3, KT, SLAB])
        consts = at("consts", 48, [P, C_END])
        small_b = at("small_b", 54.8, [P, 8])
        gates_in = at("gates_in", 54.85, [P, 3, 32])
        g_li = at("g_li", 55.25, [32, P])
        g_b = at("g_b", 55.75, [32, P])
        g_r = at("g_r", 56.25, [32, P])
        g_g = at("g_g", 56.75, [32, P])
        g_ng = at("g_ng", 57.25, [32, P])
        g_e1 = at("g_e1", 57.75, [32, P])
        g_e2 = at("g_e2", 58.25, [32, P])
        g_w = at("g_w", 58.75, [32, P])
        g_tmp = at("g_tmp", 59.25, [32, P])
        g_rowbuf = at("g_rowbuf", 59.75, [1, 4, 32])
        g_col = at("g_col", 60.25, [32, 4])
        g_diag = at("g_diag", 60.375, [32, 32])
        gate_cols = at("gate_cols", 60.5, [P, 5, 32])
        rms_tmp = at("rms_tmp", 61.25, [P, 3, 8])
        att_m = at("att_m", 61.5, [P, 3, 4])
        att_bias = at("att_bias", 61.6, [P, 3])
        att_sum = at("att_sum", 61.65, [P, 2, 8])
        att_rec = at("att_rec", 61.75, [P, 8])
        top8 = at("top8", 61.8, [P, 8])
        m_stat = at("m_stat", 61.85, [P, 4, 6])
        m_mv = at("m_mv", 61.95, [P, NT, 4, 2])
        m_rstd = at("m_rstd", 62.25, [P, NT, 4])
        m_nmr = at("m_nmr", 62.4, [P, NT, 4])
        m_den = at("m_den", 62.6, [P, 2, 4])
        ln_stat = at("ln_stat", 62.65, [P, 2, 2, 6])
        ln_mv = at("ln_mv", 62.75, [P, 2, 2])
        ln_rstd = at("ln_rstd", 62.8, [P, 2, 2])
        X = 64
        xT = at("xT", X, [P, KT, S])
        catT = at("catT", X, [P, KT, S])
        qiT = at("qiT", X + 32, [P, 4, S])
        kiT = at("kiT", X + 48, [P, S])
        score = at("score", X + 52, [P, 36 * P])
        qaT = at("qaT", X + 70, [P, 4, S])
        ucT = at("ucT", X + 86, [P, 4, S])
        vaug = at("vaug", X + 102, [P, NT, 4, MD + 1])
        zs = at("zs", X + 118.5, [P, NT, 4, MD])
        Vn = at("Vn", X + 102, [P, NT, AH * AD])
        KTr = at("KTr", X + 118.5, [P, 4, S])
        sm = at("sm", X + 134.5, [P, NT, SMALL])
        cT = at("cT", X + 139.1, [P, S])
        rel = at("rel", X + 86, [P, 2, S])
        uT = at("uT", X + 32, [P, 4, S + 3])
        normg = at("normg", X + 48.5, [P, 512])
        convw = at("convw", 63.7, [P, 4, 5])
        g_kv = at("g_kv", 63.9, [P, 1])
        mqk = at("mqk", X + 32, [P, 3, 4, MD])
        ma = at("ma", X + 38, [P, 4, P])
        mwv = at("mwv", X + 40, [P, 4, MD + 1])
        mnum = at("mnum", X + 42.1, [P, 4, MD + 1])
        mst = at("mst", X + 44.2, [P, 4, MD + 1])
        mC = at("mC", X + 46.3, [P, 4, MD + 1])
        w_m = at("w_m", X + 66, [P, 2, 4, MD])
        Lp = at("Lp", X + 32, [P, 3, S])
        pT = at("pT", X + 44, [P, 2, NT, P])
        ao = at("ao", X + 134.5, [P, 512])
        w_ukv = at("w_ukv", X, [P, 2, 512])
        w_m = at("w_m", X + 4, [P, 2, 4, MD])
        h1all = at("h1all", X + 70, [P, NT, D])
        lnp = at("lnp", X + 32, [P, 2, D])
        h1T = at("h1T", X + 40, [P, 2, KT, P])
        bdown = at("bdown", X + 48, [NE, D])
        GT = at("GT", X + 52, [NE, S])
        accst = at("accst", X + 56, [P, 2, D])
        w_rt = at("w_rt", X + 64, [P, KT, NE])
        br = at("br", X + 65, [P, NE])
        lgT = at("lgT", X + 65.25, [NE, 2, P])
        lg = at("lg", X + 66.25, [P, NT, NE])
        top_v = at("top_v", X + 67.25, [P, NT, 8])
        top_i = at("top_i", X + 67.5, [P, NT, 8], u32)
        idxf = at("idxf", X + 67.75, [P, NT, 4])
        gexp = at("gexp", X + 68, [P, NT, 4])
        gsum = at("gsum", X + 68.25, [P, 2, NT])
        hot = at("hot", X + 134.5, [P, NT, 4, NE])
        rt_t = at("rt_t", X + 138.5, [P, 10, NE])
        rt_c = at("rt_c", X + 140, [P, 12])
        rt_row = at("rt_row", X + 140.5, [1, 4, MAX_ITEMS])
        gslot = at("gslot", 55.25, [P, NT, NE])
        gates = at("gates", 56.25, [P, NT, NE])
        picks = at("picks", 57.25, [P, NT, NE])
        tot = at("tot", 58.25, [P, NT, NE])
        base = at("base", 59.25, [P, NT, NE])
        picks_b = at("picks_b", 60.25, [P, NT, NE], bf16)
        table = at("table", 61, [1, 4 * MAX_ITEMS], i32)
        cb = at("cb", 63, [P, 2 * P + 24], bf16)
        whi = at("whi", X + 102, [P, 2, KT, SLAB], f32r)
        wlo = at("wlo", X, [P, 2, KT, SLAB], f32r)
        xhi = at("xhi", X + 32, [P, KT, CAP], f32r)
        xlo = at("xlo", X + 40, [P, KT, CAP], f32r)
        hhi = at("hhi", X + 48, [P, KT, CAP], f32r)
        hlo = at("hlo", X + 56, [P, KT, CAP], f32r)
        hb = at("hb", X + 64, [P, 2, D])
        xg = at("xg", X + 72, [P, 2, HROW])
        ysb = at("ysb", X + 80.5, [P, 2, D])
        slots = at("slots", X + 88.5, [P, NT, CAP], bf16)
        gu = at("gu", X + 92.5, [P, 2, 2, SLAB])
        bgu = at("bgu", X + 134.5, [P, 2 * D])
        relv = at("relv", 62, [P, NT])
        slot_n = at("slot_n", 62.05, [P, 2, 3])
        slot_a = at("slot_a", 62.1, [P, 2, 2])
        idx_next = at("idx_next", 62.15, [P, 2], u32)
        idx_cur = at("idx_cur", 62.2, [P, 2], u32)
        gcol = at("gcol", 62.25, [P, 2])
        fin = at("fin", X + 102, [P, NT, D])
        lnq = at("lnq", X, [P, 2, D])
        fstat = at("fstat", X + 8, [P, NT, 2, 6])
        fmv = at("fmv", X + 9, [P, NT, 2])
        frs = at("frs", X + 9.25, [P, 2, NT])

        ps = [ctx.enter_context(nc.psum_tensor(f"ps{n}", [P, 512], f32)) for n in range(8)]
        hext = nc.dram_tensor("hext", [S, HROW], f32, kind="Internal").ap()
        acc = nc.dram_tensor("acc", [S, D], f32, kind="Internal").ap()

        ident = consts[:, C_ID:C_ID + P]
        cmask = consts[:, C_MASK:C_MASK + P]
        onesf = consts[:, C_ONE:C_ONE + P]
        iota_e = consts[:, C_IOTA:C_IOTA + NE]
        slab_slot = lambda q: q % 3

        def score_of(t):
            o = P * t * (t + 1) // 2
            return score[:, o:o + P * (t + 1)]

        def dist_of(t):
            return consts[:, C_DIST + S - P * (t + 1):C_DIST + S]

        def gate_at(k, c):
            return gate_cols[:, k, :].rearrange("p (h c) -> p h c", h=4)[:, :, c]

        full = [sem(f"bank_full{n}") for n in range(NB)]
        out_of = [sem(f"bank_copied{n}") for n in range(NB)]

        def bank(task):
            return ps[PLACE[task][0]]

        def filled(eng, task):
            b, u = PLACE[task]
            eng.wait_ge(full[b], u + 1)
            return ps[b]

        def copied(eng, task):
            b, u = PLACE[task]
            eng.wait_ge(out_of[b], u + 1)

        def frees(ins, task):
            ins.then_inc(out_of[PLACE[task][0]], 1)

        def serial(eng, s):
            n = [0]

            def step(ins):
                ins.then_inc(s, 1)
                n[0] += 1
                eng.wait_ge(s, n[0])
            return step

        x_in = [sem(f"x_in{n}") for n in range(2)]
        raw_in = [sem(f"raw_in{n}") for n in range(3)]
        consts_in, bias_in, wm_in, late_in, normg_in = (
            sem("consts_in"), sem("bias_in"), sem("wm_in"), sem("late_in"), sem("normg_in"))
        xres_in, lnp_in, lnq_in = sem("xres_in"), sem("lnp_in"), sem("lnq_in")
        score_acc, gates_cp = sem("score_acc"), sem("gates_cp")
        topk_step, gate_step, rms_step, ml_step = sem("topk_step"), sem("gate_step"), sem("rms_step"), sem("ml_step")
        lf_in, lf_exp, lf_ln, lf_done = sem("lf_in"), sem("lf_exp"), sem("lf_ln"), sem("lf_done")
        rows_done, mrow_done, g_done, gexp_step, gexp_done, diag_done = (
            sem("rows_done"), sem("mrow_done"), sem("g_done"), sem("gexp_step"), sem("gexp_done"), sem("diag_done"))
        rms_sum, rms_root, rms_done = sem("rms_sum"), sem("rms_root"), sem("rms_done")
        pad_set, conv_step, conv_done, uc_ready = sem("pad_set"), sem("conv_step"), sem("conv_done"), sem("uc_ready")
        ones_set, zgated = sem("ones_set"), sem("zgated")
        gate_exp, wv_done, c_decayed, x_part, h_written = (
            sem("gate_exp"), sem("wv_done"), sem("c_decayed"), sem("x_part"), sem("h_written"))
        mvar_done, mroot, mnorm_in, mnormed, mout = (
            sem("mvar_done"), sem("mroot"), sem("mnorm_in"), sem("mnormed"), sem("mout"))
        att_shift, p_ready, o_full, o_copied, att_step = (
            sem("att_shift"), sem("p_ready"), sem("o_full"), sem("o_copied"), sem("att_step"))
        ln_step, ln_var, ln_root, ln_sb, ln_norm, h1_done = (
            sem("ln_step"), sem("ln_var"), sem("ln_root"), sem("ln_sb"), sem("ln_norm"), sem("h1_done"))
        rt_step, rt_diff, rt_exp, picks_done, items_done, table_done = (
            sem("rt_step"), sem("rt_diff"), sem("rt_exp"), sem("picks_done"), sem("items_done"), sem("table_done"))
        gates_done, acc_half, h_out, acc_out, gate_out = (
            sem("gates_done"), sem("acc_half"), sem("h_out"), [sem(f"acc_out{n}") for n in range(2)], sem("gate_out"))
        hi_done, lo_part, lo_done, slab_used = sem("hi_done"), sem("lo_part"), sem("lo_done"), sem("slab_used")
        gu_full1 = sem("gu_full1")
        g_read = [sem(f"g_read{b}") for b in range(2)]
        u_read = [sem(f"u_read{b}") for b in range(2)]
        sig_done = [sem(f"sig_done{b}") for b in range(2)]
        clip_g = [sem(f"clip_g{b}") for b in range(2)]
        clip_u = [sem(f"clip_u{b}") for b in range(2)]
        up_done = [sem(f"up_done{b}") for b in range(2)]
        hb_done = [sem(f"hb_done{b}") for b in range(2)]
        tr_full = [sem(f"tr_full{b}") for b in range(2)]
        tr_hi = [sem(f"tr_hi{b}") for b in range(2)]
        tr_free = [sem(f"tr_free{b}") for b in range(2)]
        y_full1 = sem("y_full1")
        y_done = [sem(f"y_done{b}") for b in range(2)]
        gathered = [sem(f"gathered{b}") for b in range(2)]
        added = [sem(f"added{b}") for b in range(2)]
        gate_cp, idx_step, idx_done, slots_done, rel_done, idx_kept, bgu_in = (
            sem("gate_cp"), sem("idx_step"), sem("idx_done"), sem("slots_done"), sem("rel_done"),
            sem("idx_kept"), sem("bgu_in"))
        tokens_in = sem("tokens_in")
        pool_passed, act_passed = sem("pool_passed"), sem("act_passed")
        xg_set, all_added = sem("xg_set"), sem("all_added")
        fin_in, f_step, f_var, f_root, f_sb, f_norm, f_done, f_out = (
            [sem(f"fin_in{n}") for n in range(2)], sem("f_step"), sem("f_var"), sem("f_root"), sem("f_sb"), sem("f_norm"),
            sem("f_done"), sem("f_out"))

        last_use = [("qi", 3, 1), ("small", 3), ("qa", 3, 1), ("u", 3, 1), ("v", NT - 1), ("z", NT - 1),
                    ("mix", NT - 1, 0), ("mix", NT - 1, 1)]
        last_sc = ("sc", NT - 1, AH - 1, 1)
        NPRE = len(last_use)
        n_sc = (NT - 2) * AH

        def item_table(eng):
            def entry(row, i, top):
                return eng.value_load(table[0:1, bass.ds(i + row * MAX_ITEMS, 1)], min_val=0, max_val=top)
            return entry

        def since(n):
            return n + 1

        def starts(eng, sems):
            for s in sems:
                eng.sem_inc(s, 1)

        block = ctx.enter_context(nc.Block())

        @block.sync
        def _(sp):
            def slab(q, src, width=SLAB):
                if q >= 3:
                    filled(sp, last_use[q - 3])
                sp.dma_start(raw[:, slab_slot(q), :, 0:width], src).then_inc(raw_in[slab_slot(q)], 16)

            sp.dma_start(xT[:, :, 0:512], a["xT"][:, :, 0:512]).then_inc(x_in[0], 16)
            slab(0, a["w_qi"])
            sp.dma_start(xT[:, :, 512:S], a["xT"][:, :, 512:S]).then_inc(x_in[1], 16)
            slab(1, a["w_ks"], P + SMALL)
            slab(2, a["w_qa"])
            slab(3, a["w_u"])
            slab(4, a["w_v"])
            slab(5, a["w_z"])
            filled(sp, ("z", NT - 1))
            sp.dma_start(w_ukv[:, :, :], a["w_ukv"]).then_inc(wm_in, 16)
            sp.dma_start(w_m[:, :, :, :], a["w_m"]).then_inc(wm_in, 16)
            slab(6, a["w_out"][0])
            slab(7, a["w_out"][1])
            slab(8, a["w_gu"][0])
            filled(sp, ("L", NT * AH - 1, 1))
            copied(sp, ("L", NT * AH - 1, 1))
            for g in range(4):
                sp.dma_start(h1all[:, 2 * g:2 * g + 2, :], a["x"][:, 2 * g:2 * g + 2, :]).then_inc(xres_in, 16)
            for q in range(9, 11):
                filled(sp, last_use[q - 3])
                sp.dma_start(raw[:, slab_slot(q), :, :], a["w_gu"][q - NPRE]).then_inc(raw_in[slab_slot(q)], 16)
            for t in range(NT):
                sp.wait_ge(h1_done, t + 1)
                sp.dma_start(hext[t * P:(t + 1) * P, 0:D], h1all[:, t, :]).then_inc(h_out, 16)
            sp.wait_ge(gates_done, 1)
            sp.dma_start(hext[:, D:HROW].rearrange("(t p) e -> p t e", p=P), gates[:, :, :]).then_inc(gate_out, 16)
            for t in range(NT):
                sp.wait_ge(acc_half, t + 1)
                sp.dma_start(acc[t * P:(t + 1) * P, :], accst[:, t % 2, :]).then_inc(acc_out[t % 2], 16)
            for j in range(3, 6):
                sp.wait_ge(lo_done, j - 2)
                src = a["w_gu"][j] if j < 4 else a["w_dn"][j - 4]
                sp.dma_start(raw[:, (j + 2) % 3, :, :], src).then_inc(raw_in[(j + 2) % 3], 16)
            sp.wait_ge(table_done, 1)
            entry = item_table(sp)
            n = sp.value_load(table[0:1, 3 * MAX_ITEMS:3 * MAX_ITEMS + 1], min_val=NE, max_val=MAX_ITEMS)
            with sp.Fori(1, n) as i:
                e = entry(0, i, NE - 1)
                for j in range(6):
                    sp.wait_ge(lo_done, 6 * i + (j - 2))
                    src = a["w_gu"][bass.ds(e * 4 + j, 1)] if j < 4 else a["w_dn"][bass.ds(e * 2 + (j - 4), 1)]
                    sp.dma_start(raw[:, (j + 2) % 3, :, :], src.rearrange("o p k c -> p (o k) c")).then_inc(raw_in[(j + 2) % 3], 16)
            sp.wait_ge(all_added, 1)
            for g in range(2):
                sp.dma_start(fin[:, 4 * g:4 * g + 4, :],
                             acc[g * 512:(g + 1) * 512, :].rearrange("(t p) d -> p t d", p=P)).then_inc(fin_in[g], 16)
            for t in range(NT):
                sp.wait_ge(f_done, t + 1)
                sp.dma_start(out[0, t * P:(t + 1) * P, :], fin[:, t, :]).then_inc(f_out, 16)
            sp.wait_ge(f_out, 16 * NT)

        @block.tensor
        def _(pe):
            def opened(task):
                b, u = PLACE[task]
                if u:
                    pe.wait_ge(out_of[b], u)
                return ps[b]

            def closes(ins, task):
                ins.then_inc(full[PLACE[task][0]], 1)

            def slab_ready(q):
                pe.wait_ge(raw_in[slab_slot(q)], 16 * (q // 3 + 1))
                return raw[:, slab_slot(q), :, :]

            def feature_major(name, q, order=tuple((m, n) for n in range(2) for m in range(4))):
                w = slab_ready(q)
                for m, n in order:
                    if name == "qi" and m == 0:
                        pe.wait_ge(x_in[n], 16)
                    task = (name, m, n) if name != "ki" else (name, n)
                    b = opened(task)
                    for k in range(KT):
                        ins = pe.matmul(b[:, :], w[:, k, m * P:(m + 1) * P], xT[:, k, n * 512:(n + 1) * 512],
                                        start=k == 0, stop=k == KT - 1)
                    closes(ins, task)

            def token_major(name, q, col, width, per_bank):
                w = slab_ready(q)
                for j in range(NT // per_bank):
                    b = opened((name, j))
                    for i in range(per_bank):
                        t = j * per_bank + i
                        for k in range(KT):
                            ins = pe.matmul(b[:, i * width:(i + 1) * width], xT[:, k, t * P:(t + 1) * P],
                                            w[:, k, col:col + width], start=k == 0, stop=k == KT - 1)
                    closes(ins, (name, j))

            pe.wait_ge(consts_in, 32)
            feature_major("qi", 0)
            feature_major("ki", 1, [(0, 0), (0, 1)])
            token_major("small", 1, P, SMALL, 2)
            for n in range(2):
                for m in range(4):
                    copied(pe, ("qi", m, n))
                copied(pe, ("ki", n))
            for t in range(2, NT):
                for h in range(AH):
                    lo, m = AD * (h % 2), h // 2
                    for c, (k0, k1) in enumerate(chunks(t)):
                        b = opened(("sc", t, h, c))
                        closes(pe.matmul(b[:, 0:k1 - k0], qiT[lo:lo + AD, m, t * P:(t + 1) * P],
                                         kiT[lo:lo + AD, k0:k1], start=True, stop=True), ("sc", t, h, c))
            b = opened(("grow",))
            pe.wait_ge(lf_done, 1)
            pe.transpose(b[0:32, 0:P], gates_in[:, 0, :], ident)
            closes(pe.transpose(b[0:32, P:2 * P], gates_in[:, 2, :], ident), ("grow",))
            feature_major("qa", 2)
            b = opened(("grow2",))
            pe.wait_ge(rows_done, 1)
            pe.transpose(b[0:1, 0:32], g_b[:, P - 1:P], ident[0:32, 0:32])
            closes(pe.transpose(b[0:1, 32:64], g_tmp[:, P - 1:P], ident[0:32, 0:32]), ("grow2",))
            b = opened(("mprev",))
            pe.wait_ge(mrow_done, 1)
            closes(pe.matmul(b[0:32, 0:2], g_rowbuf[:, 3, :], onesf[0:1, 0:2], start=True, stop=True), ("mprev",))
            feature_major("u", 3)
            b = opened(("gcol",))
            pe.wait_ge(gexp_done, 1)
            pe.wait_ge(diag_done, 1)
            for k, rows in enumerate((g_r, g_e1, g_e2, g_w)):
                pe.transpose(b[:, 32 * k:32 * k + 32], rows[:, :], ident[0:32, 0:32])
            closes(pe.matmul(b[:, 128:160], onesf[0:32, :], g_diag[:, :], start=True, stop=True), ("gcol",))
            token_major("v", 4, 0, SLAB, 1)
            token_major("z", 5, 0, SLAB, 1)
            pe.wait_ge(rms_done, 1)
            for j in range(2):
                b = opened(("ct", j))
                for i in range(4):
                    ins = pe.transpose(b[:, i * P:(i + 1) * P], sm[:, 4 * j + i, 0:R], ident)
                closes(ins, ("ct", j))
            pe.wait_ge(wm_in, 32)
            pe.wait_ge(uc_ready, 4)
            copied(pe, ("gcol",))
            for c in range(NT):
                tok = slice(c * P, (c + 1) * P)
                for k, name in enumerate(("mq", "mk", "mkt")):
                    b = opened((name, c))
                    for h in range(MH):
                        w, u = w_m[:, min(k, 1), h, :], ucT[:, h, tok]
                        ins = pe.matmul(b[:, h * P:(h + 1) * P], w if k < 2 else u, u if k < 2 else w,
                                        start=True, stop=True)
                    closes(ins, (name, c))
                b = opened(("R", c))
                for h in range(MH):
                    row = ident[0:32, h * 8 + c:h * 8 + c + 1].to_broadcast([32, P])
                    ins = pe.matmul(b[:, h * P:(h + 1) * P], row, g_ng[:, :], start=True, stop=True)
                closes(ins, ("R", c))
                b = opened(("S", c))
                copied(pe, ("mq", c))
                copied(pe, ("mk", c))
                for h in range(MH):
                    ins = pe.matmul(b[:, h * P:(h + 1) * P], mqk[:, 1, h, :], mqk[:, 0, h, :], start=True, stop=True)
                closes(ins, ("S", c))
                for q in range(2 if c else 0):
                    b = opened(("X", c, q))
                    copied(pe, ("U", c - 1, q))
                    for h in (2 * q, 2 * q + 1):
                        ins = pe.matmul(b[:, (h % 2) * 129:(h % 2) * 129 + 129], mqk[:, 0, h, :], mC[:, h, :],
                                        start=True, stop=True)
                    closes(ins, ("X", c, q))
                copied(pe, ("v", c))
                pe.wait_ge(ones_set, 1)
                copied(pe, ("S", c))
                for q in range(2):
                    b = opened(("I", c, q))
                    for h in (2 * q, 2 * q + 1):
                        ins = pe.matmul(b[:, (h % 2) * 129:(h % 2) * 129 + 129], ma[:, h, :], vaug[:, c, h, :],
                                        start=True, stop=True)
                    closes(ins, ("I", c, q))
                for q in range(2 if c < NT - 1 else 0):
                    b = opened(("U", c, q))
                    copied(pe, ("mkt", c))
                    pe.wait_ge(wv_done, c + 1)
                    for h in (2 * q, 2 * q + 1):
                        ins = pe.matmul(b[:, (h % 2) * 129:(h % 2) * 129 + 129], mqk[:, 2, h, :], mwv[:, h, :],
                                        start=True, stop=True)
                    closes(ins, ("U", c, q))
            for c in range(NT):
                b = opened(("mt", c))
                pe.wait_ge(mout, c + 1)
                for h in range(MH):
                    ins = pe.transpose(b[:, h * P:(h + 1) * P], zs[:, c, h, :], ident)
                closes(ins, ("mt", c))
            for j in range(2):
                copied(pe, ("ct", j))
            for n in range(2):
                for m in range(4):
                    b = opened(("kt", m, n))
                    closes(pe.matmul(b[:, :], w_ukv[:, 0, m * P:(m + 1) * P], cT[:, n * 512:(n + 1) * 512],
                                     start=True, stop=True), ("kt", m, n))
            for t in range(NT):
                b = opened(("V", t))
                closes(pe.matmul(b[:, :], cT[:, t * P:(t + 1) * P], w_ukv[:, 1, :], start=True, stop=True), ("V", t))
            for n in range(2):
                for m in range(4):
                    copied(pe, ("kt", m, n))
            for n in range(NT * AH + 4):
                if n < NT * AH:
                    t, h = divmod(n, AH)
                    lo, m = AD * (h % 2), h // 2
                    for c, (k0, k1) in enumerate(chunks(t)):
                        b = opened(("L", n, c))
                        closes(pe.matmul(b[:, 0:k1 - k0], qaT[lo:lo + AD, m, t * P:(t + 1) * P],
                                         KTr[lo:lo + AD, m, k0:k1], start=True, stop=True), ("L", n, c))
                if 1 <= n <= NT * AH:
                    pe.wait_ge(p_ready, n)
                    for g, (j0, j1) in enumerate(groups((n - 1) // AH)):
                        b = opened(("T", n - 1, g))
                        for j in range(j0, j1):
                            ins = pe.transpose(b[:, (j - j0) * P:(j - j0 + 1) * P],
                                               Lp[:, (n - 1) % 3, j * P:(j + 1) * P], ident)
                        closes(ins, ("T", n - 1, g))
                if 2 <= n < NT * AH + 2:
                    t, h = divmod(n - 2, AH)
                    if h == 0:
                        copied(pe, ("V", t))
                        if t:
                            pe.wait_ge(o_copied, t)
                    for g in range(len(groups(t))):
                        copied(pe, ("T", n - 2, g))
                    for j in range(t + 1):
                        ins = pe.matmul(ps[NB][:, h * AD:(h + 1) * AD], pT[:, (n - 2) % 2, j, :],
                                        Vn[:, j, h * AD:(h + 1) * AD], start=j == 0, stop=j == t)
                    if h == AH - 1:
                        ins.then_inc(o_full, 1)
                if n >= 11 and n % AH == 3:
                    t = n // AH - 1
                    b = opened(("at", t))
                    pe.wait_ge(o_copied, t + 1)
                    for j in range(4):
                        ins = pe.transpose(b[:, j * P:(j + 1) * P], ao[:, j * P:(j + 1) * P], ident)
                    closes(ins, ("at", t))

            def mix(t):
                for n in range(2):
                    w = slab_ready(6 + n)
                    b = opened(("mix", t, n))
                    for k in range(KT):
                        ins = pe.matmul(b[:, :], catT[:, k, t * P:(t + 1) * P], w[:, k, :],
                                        start=k == 0, stop=k == KT - 1)
                    closes(ins, ("mix", t, n))

            def h_turned(t):
                pe.wait_ge(h1_done, t + 1)
                for g in range(2):
                    b = opened(("ht", t, g))
                    for k in range(4):
                        ins = pe.transpose(b[:, k * P:(k + 1) * P], h1all[:, t, (4 * g + k) * P:(4 * g + k + 1) * P],
                                           ident)
                    closes(ins, ("ht", t, g))

            def router(t):
                b = opened(("rt", t))
                for g in range(2):
                    copied(pe, ("ht", t, g))
                for k in range(KT):
                    ins = pe.matmul(b[0:NE, 0:P], w_rt[:, k, :], h1T[:, t % 2, k, :], start=k == 0, stop=k == KT - 1)
                closes(ins, ("rt", t))
                b = opened(("rtt", t))
                copied(pe, ("rt", t))
                closes(pe.transpose(b[:, 0:NE], lgT[:, t % 2, :], ident[0:NE, 0:NE]), ("rtt", t))

            for t in range(NT):
                copied(pe, ("at", t))
                copied(pe, ("mt", t))
            pe.wait_ge(lnp_in, 80)
            for t in range(NT):
                mix(t)
                if t:
                    h_turned(t - 1)
                if t > 1:
                    router(t - 2)
            h_turned(NT - 1)
            router(NT - 2)
            router(NT - 1)
            b = opened(("cnt",))
            pe.wait_ge(picks_done, 1)
            pe.matmul(b[:, 0:256], cb[:, 0:P], picks_b[:, :, :].rearrange("p t e -> p (t e)"), start=True, stop=True)
            closes(pe.matmul(b[:, 256:512], cb[:, P:2 * P], picks_b[:, :, :].rearrange("p t e -> p (t e)"),
                             start=True, stop=True), ("cnt",))
            b = opened(("items",))
            pe.wait_ge(items_done, 1)
            pe.transpose(b[0:1, 0:P], rt_c[:, 0:1], ident)
            closes(pe.transpose(b[0:1, P:2 * P], rt_c[:, 1:2], ident), ("items",))
            for j in range(2):
                b = opened(("gt", j))
                for i in range(4):
                    ins = pe.transpose(b[0:NE, i * P:(i + 1) * P], gates[:, 4 * j + i, :], ident)
                closes(ins, ("gt", j))
            for t in range(NT):
                copied(pe, ("gt", t // 4))
                for n in range(2):
                    b = opened(("bd", t, n))
                    closes(pe.matmul(b[:, :], GT[:, t * P:(t + 1) * P], bdown[:, n * 512:(n + 1) * 512],
                                     start=True, stop=True), ("bd", t, n))

            for b in range(NB):
                pe.wait_ge(out_of[b], len([1 for v in PLACE.values() if v[0] == b]))
            pe.wait_ge(table_done, 1)
            entry = item_table(pe)
            n_items = pe.value_load(table[0:1, 3 * MAX_ITEMS:3 * MAX_ITEMS + 1], min_val=NE, max_val=MAX_ITEMS)

            def halves(bank_ap, lhs_hi, lhs_lo, slot, ks, first, last):
                for k in ks:
                    pe.matmul(bank_ap, lhs_hi[k], whi[:, slot, k, :], start=first and k == ks[0], stop=False)
                    pe.matmul(bank_ap, lhs_hi[k], wlo[:, slot, k, :], start=False, stop=False)
                    ins = pe.matmul(bank_ap, lhs_lo[k], whi[:, slot, k, :], start=False, stop=last and k == ks[-1])
                return ins

            def lhs(hi_buf, lo_buf, b):
                return ([hi_buf[:, k, b * P:(b + 1) * P] for k in range(KT)],
                        [lo_buf[:, k, b * P:(b + 1) * P] for k in range(KT)])

            def find_slots(item, fills):
                pe.wait_ge(slots_done, item + 1)
                pe.wait_ge(tr_free[0], since(fills))
                for b in range(2):
                    for t in range(NT):
                        ins = pe.matmul(ps[4][:, 4 * b:4 * b + 3], slots[:, t, b * P:(b + 1) * P],
                                        cb[:, 2 * P + 3 * t:2 * P + 3 * t + 3], start=t == 0, stop=t == NT - 1)
                ins.then_inc(tr_full[0], 1)

            def turn(b, src, fills, free_at):
                for f, g in enumerate(fills):
                    pe.wait_ge(tr_free[b], since(free_at + f))
                    for k in range(4):
                        ins = pe.transpose(ps[4 + b][:, k * P:(k + 1) * P],
                                           src[:, b, (4 * g + k) * P:(4 * g + k + 1) * P], ident)
                    ins.then_inc(tr_full[b], 1)

            starts(pe, tr_full)
            find_slots(0, 0)
            b1_0 = entry(1, 0, 1)
            with pe.If(b1_0 > 0):
                pe.wait_ge(gathered[1], 16)
                turn(1, xg, (0, 1), 0)
            pe.wait_ge(gathered[0], 16)
            turn(0, xg, (0, 1), 1)
            with pe.Fori(0, n_items) as i:
                b1, n1 = entry(1, i, 1), entry(2, i, MAX_ITEMS)
                b1x, n1x = entry(1, i + 1, 1), entry(2, i + 1, MAX_ITEMS)
                find_slots(i + 1, i * 5 + 3)
                for j in range(4):
                    pe.wait_ge(lo_done, i * 6 + (j + 1))
                    if j == 0:
                        pe.wait_ge(tr_free[0], since(i * 5 + 3))
                    with pe.If(b1 > 0):
                        if j == 0:
                            pe.wait_ge(tr_free[1], since(n1 * 4 + 2))
                            pe.wait_ge(y_done[1], since(n1 * 2))
                        read = (g_read, u_read)[j % 2][1]
                        pe.wait_ge(read, since(n1 * 2 + j // 2))
                        halves(ps[2 + j % 2][:, :], *lhs(xhi, xlo, 1), j % 2, list(range(KT)), True, True).then_inc(gu_full1, 1)
                    pe.wait_ge((g_read, u_read)[j % 2][0], since(i * 2 + j // 2))
                    halves(ps[j % 2][:, :], *lhs(xhi, xlo, 0), j % 2, list(range(KT)), True, True).then_inc(slab_used, 1)
                    if j == 2:
                        with pe.If(b1 > 0):
                            pe.wait_ge(hb_done[1], since(n1 * 2 + 1))
                            turn(1, hb, (0,), n1 * 4 + 2)
                        pe.wait_ge(hb_done[0], since(i * 2 + 1))
                        turn(0, hb, (0,), i * 5 + 4)
                lo4, hi4 = list(range(4)), list(range(4, 8))
                for s in range(2):
                    pe.wait_ge(lo_done, i * 6 + (5 + s))
                    if s == 0:
                        pe.wait_ge(tr_free[0], since(i * 5 + 5))
                    pe.wait_ge(y_done[0], since(i * 2))
                    halves(ps[6 + s][:, :], *lhs(hhi, hlo, 0), s, lo4, True, False)
                with pe.If(b1 > 0):
                    pe.wait_ge(tr_free[1], since(n1 * 4 + 3))
                    for s in range(2):
                        pe.wait_ge((g_read, u_read)[s][1], since(n1 * 2 + 2))
                        halves(ps[2 + s][:, :], *lhs(hhi, hlo, 1), s, lo4, True, False)
                    pe.wait_ge(hb_done[1], since(n1 * 2 + 2))
                    turn(1, hb, (1,), n1 * 4 + 3)
                pe.wait_ge(hb_done[0], since(i * 2 + 2))
                turn(0, hb, (1,), i * 5 + 5)
                with pe.If(b1x > 0):
                    pe.wait_ge(gathered[1], n1x * 16 + 16)
                    turn(1, xg, (0, 1), n1x * 4)
                pe.wait_ge(gathered[0], i * 16 + 32)
                turn(0, xg, (0, 1), i * 5 + 6)
                for s in range(2):
                    with pe.If(b1 > 0):
                        if s == 0:
                            pe.wait_ge(tr_free[1], since(n1 * 4 + 4))
                        halves(ps[2 + s][:, :], *lhs(hhi, hlo, 1), s, hi4, False, True).then_inc(y_full1, 1)
                    if s == 0:
                        pe.wait_ge(tr_free[0], since(i * 5 + 6))
                    halves(ps[6 + s][:, :], *lhs(hhi, hlo, 0), s, hi4, False, True).then_inc(slab_used, 1)

        @block.scalar
        def _(act):
            def copy_out(task, dst, src, func=ACT.Copy, **kw):
                frees(act.activation(dst, src, func, **kw), task)

            act.dma_start(consts[:, :], a["consts"]).then_inc(consts_in, 16)
            act.dma_start(cb[:, :], a["cb"]).then_inc(consts_in, 16)
            act.dma_start(small_b[:, :], a["b_if"].partition_broadcast(P)).then_inc(bias_in, 16)
            act.dma_start(g_kv[:, :], a["kv_norm_g"]).then_inc(late_in, 16)
            act.dma_start(convw[:, :, :], a["conv"]).then_inc(late_in, 16)
            act.wait_ge(consts_in, 32)
            for n in range(2):
                for m in range(4):
                    b = filled(act, ("qi", m, n))
                    copy_out(("qi", m, n), qiT[:, m, n * 512:(n + 1) * 512], b[:, :])
            for n in range(2):
                copy_out(("ki", n), kiT[:, n * 512:(n + 1) * 512], filled(act, ("ki", n))[:, :])
            act.wait_ge(lf_in, 3)
            act.activation(gates_in[:, 2, :], gates_in[:, 2, :], ACT.Exp).then_inc(lf_exp, 1)
            act.wait_ge(lf_exp, 1)
            act.activation(gates_in[:, 2, :], gates_in[:, 2, :], ACT.Ln, bias=1.0).then_inc(lf_ln, 1)
            act.wait_ge(rms_sum, NT)
            act.activation(rms_tmp[:, 1, :], rms_tmp[:, 0, :], ACT.Sqrt, scale=1.0 / R, bias=consts[:, C_COL + 1:C_COL + 2]).then_inc(rms_root, 1)
            r = 0
            for t in range(2, NT):
                for h in range(AH):
                    if r >= 2:
                        act.wait_ge(score_acc, r - 1)
                    for c, (k0, k1) in enumerate(chunks(t)):
                        b = filled(act, ("sc", t, h, c))
                        copy_out(("sc", t, h, c), rel[:, r % 2, k0:k1], b[:, 0:k1 - k0], ACT.Relu)
                    r += 1
            act.dma_start(normg[:, :], a["m_norm_g"].partition_broadcast(P)).then_inc(normg_in, 16)
            for n in range(2):
                for m in range(4):
                    b = filled(act, ("qa", m, n))
                    copy_out(("qa", m, n), qaT[:, m, n * 512:(n + 1) * 512], b[:, :], scale=consts[:, C_QS + m:C_QS + m + 1])
            for n in range(2):
                for m in range(4):
                    b = filled(act, ("u", m, n))
                    copy_out(("u", m, n), uT[:, m, 3 + n * 512:3 + (n + 1) * 512], b[:, :])
            act.wait_ge(g_done, 1)
            act.activation(g_e1[:, :], g_g[:, :], ACT.Exp, scale=-1.0, bias=g_col[:, 0:1]).then_inc(gexp_step, 1)
            act.activation(g_e2[:, :], g_tmp[:, :], ACT.Exp, scale=-1.0).then_inc(gexp_step, 1)
            act.activation(g_w[:, :], g_r[:, :], ACT.Exp, bias=g_ng[:, P - 1:P]).then_inc(gexp_step, 1)
            act.activation(g_col[:, 1:2], g_col[:, 0:1], ACT.Exp, bias=g_ng[:, P - 1:P]).then_inc(gexp_done, 1)
            for t in range(NT):
                b = filled(act, ("v", t))
                copy_out(("v", t), vaug[:, t, :, 0:MD], b[:, :].rearrange("p (h d) -> p h d", h=4))
            for m in range(4):
                act.wait_ge(conv_done, m + 1)
                act.activation(ucT[:, m, :], ucT[:, m, :], ACT.Silu, bias=convw[:, m, 4:5]).then_inc(uc_ready, 1)
            for t in range(NT):
                b = filled(act, ("z", t))
                copy_out(("z", t), zs[:, t, :, :], b[:, :].rearrange("p (h d) -> p h d", h=4), ACT.Sigmoid)
            for j in range(2):
                b = filled(act, ("ct", j))
                copy_out(("ct", j), cT[:, j * 512:(j + 1) * 512], b[:, :], scale=g_kv[:, 0:1])
            for c in range(NT):
                for k, name in enumerate(("mq", "mk", "mkt")):
                    b = filled(act, (name, c))
                    copy_out((name, c), mqk[:, k, :, :], b[:, :].rearrange("p (h d) -> p h d", h=4),
                             scale=1.0 if k == 0 else MD ** -0.5)
                copied(act, ("R", c))
                for h in range(MH):
                    act.activation(ma[:, h, :], ma[:, h, :], ACT.Exp, bias=gate_cols[:, 0, h * 8 + c:h * 8 + c + 1])\
                       .then_inc(gate_exp, 1)
                for q in range(2 if c else 0):
                    b = filled(act, ("X", c, q))
                    copied(act, ("I", c - 1, q))
                    h = 2 * q
                    act.activation(mst[:, h, :], b[:, 0:129], ACT.Copy, scale=gate_cols[:, 1, h * 8 + c:h * 8 + c + 1])\
                       .then_inc(x_part, 1)
                    h = 2 * q + 1
                    copy_out(("X", c, q), mst[:, h, :], b[:, 129:258], scale=gate_cols[:, 1, h * 8 + c:h * 8 + c + 1])
            act.wait_ge(mvar_done, 1)
            act.activation(m_rstd[:, :, :], m_rstd[:, :, :], ACT.Sqrt).then_inc(mroot, 1)
            act.wait_ge(mnorm_in, 2)
            for c in range(NT):
                for h in range(MH):
                    act.activation(vaug[:, c, h, 0:MD], vaug[:, c, h, 0:MD], ACT.Identity,
                                   scale=m_rstd[:, c, h:h + 1], bias=m_nmr[:, c, h:h + 1]).then_inc(mnormed, 1)
            for c in range(NT):
                b = filled(act, ("mt", c))
                copy_out(("mt", c), catT[:, 4:8, c * P:(c + 1) * P], b[:, :].rearrange("p (h d) -> p h d", h=4))
            for n in range(2):
                for m in range(4):
                    copy_out(("kt", m, n), KTr[:, m, n * 512:(n + 1) * 512], filled(act, ("kt", m, n))[:, :])
            for t in range(NT):
                copy_out(("V", t), Vn[:, t, :], filled(act, ("V", t))[:, :])
            for n in range(NT * AH + 4):
                if n < NT * AH:
                    t, h = divmod(n, AH)
                    act.wait_ge(att_shift, n + 1)
                    act.activation(Lp[:, n % 3, 0:P * (t + 1)], Lp[:, n % 3, 0:P * (t + 1)], ACT.Exp,
                                   scale=2.0 ** -(h + 1), bias=att_bias[:, n % 3:n % 3 + 1],
                                   accum_out=att_sum[:, t % 2, h:h + 1]).then_inc(p_ready, 1)
                if 1 <= n <= NT * AH:
                    j0, j1 = groups((n - 1) // AH)[0]
                    b = filled(act, ("T", n - 1, 0))
                    copy_out(("T", n - 1, 0), pT[:, (n - 1) % 2, j0:j1, :],
                             b[:, 0:(j1 - j0) * P].rearrange("p (j q) -> p j q", q=P))
                if n >= 11 and n % AH == 3:
                    t = n // AH - 1
                    b = filled(act, ("at", t))
                    copy_out(("at", t), catT[:, 0:4, t * P:(t + 1) * P], b[:, :].rearrange("p (j q) -> p j q", q=P))
            act.dma_start(lnp[:, 0, :], a["ln1_g"].partition_broadcast(P)).then_inc(lnp_in, 16)
            act.dma_start(lnp[:, 1, :], a["ln1_b"].partition_broadcast(P)).then_inc(lnp_in, 16)
            act.dma_start(bdown[:, :], a["b_down"]).then_inc(lnp_in, 16)
            act.dma_start(w_rt[:, :, :], a["w_router"]).then_inc(lnp_in, 16)
            act.dma_start(br[:, :], a["b_router"].partition_broadcast(P)).then_inc(lnp_in, 16)

            def ln1_root(t):
                act.wait_ge(ln_var, t + 1)
                act.activation(ln_rstd[:, t % 2, 0:1], ln_mv[:, t % 2, 1:2], ACT.Sqrt, bias=consts[:, C_COL + 1:C_COL + 2])\
                   .then_inc(ln_root, 1)
                act.wait_ge(ln_sb, t + 1)
                act.activation(h1all[:, t, :], h1all[:, t, :], ACT.Identity, scale=ln_rstd[:, t % 2, 0:1],
                               bias=ln_rstd[:, t % 2, 1:2]).then_inc(ln_norm, 1)

            def turned(t):
                for g in range(2):
                    b = filled(act, ("ht", t, g))
                    copy_out(("ht", t, g), h1T[:, t % 2, 4 * g:4 * g + 4, :], b[:, :].rearrange("p (j q) -> p j q", q=P))

            def router_out(t):
                b = filled(act, ("rt", t))
                copy_out(("rt", t), lgT[:, t % 2, :], b[0:NE, 0:P])

            for t in range(NT):
                ln1_root(t)
                if t:
                    turned(t - 1)
                if t > 1:
                    router_out(t - 2)
            turned(NT - 1)
            router_out(NT - 2)
            router_out(NT - 1)
            act.wait_ge(rt_diff, 1)
            act.activation(gexp[:, :, :], gexp[:, :, :], ACT.Exp).then_inc(rt_exp, 1)
            for j in range(2):
                b = filled(act, ("gt", j))
                copy_out(("gt", j), GT[:, j * 512:(j + 1) * 512], b[0:NE, :])

            act.wait_ge(table_done, 1)
            entry = item_table(act)
            n_items = act.value_load(table[0:1, 3 * MAX_ITEMS:3 * MAX_ITEMS + 1], min_val=NE, max_val=MAX_ITEMS)

            def biases(e, seen0, seen1):
                act.wait_ge(u_read[0], since(seen0))
                act.wait_ge(u_read[1], since(seen1))
                act.dma_start(bgu[:, :], a["b_gu"][bass.ds(e, 1), :].rearrange("o c -> (o c)").partition_broadcast(P))\
                   .then_inc(bgu_in, 16)

            def take_hi(j, slab, in_count):
                act.wait_ge(raw_in[(j + 2) % 3], in_count)
                for g in range(4):
                    act.activation(whi[:, j % 2, 2 * g:2 * g + 2, :], raw[:, (j + 2) % 3, 2 * g:2 * g + 2, :], ACT.Copy)\
                       .then_inc(hi_done, 1)

            def turned_hi(b, dst, g, fills):
                act.wait_ge(tr_full[b], since(fills))
                act.activation(dst[:, 4 * g:4 * g + 4, b * P:(b + 1) * P], ps[4 + b][:, :].rearrange("p (k q) -> p k q", q=P),
                               ACT.Copy).then_inc(tr_hi[b], 1)

            def sigmoid(b, half, count):
                act.wait_ge(clip_g[b], count)
                act.activation(hb[:, b, half * SLAB:(half + 1) * SLAB], gu[:, b, 0, :], ACT.Sigmoid, scale=1.702)\
                   .then_inc(sig_done[b], 1)

            def y_out(b, s):
                bk = ps[6 + s] if b == 0 else ps[2 + s]
                act.activation(ysb[:, b, s * SLAB:(s + 1) * SLAB], bk[:, :], ACT.Copy, scale=gcol[:, b:b + 1])\
                   .then_inc(y_done[b], 1)

            starts(act, y_done)
            act.dma_start(bgu[:, :], a["b_gu"][0:1, :].rearrange("o c -> (o c)").partition_broadcast(P)).then_inc(bgu_in, 16)
            for b in range(NB):
                act.wait_ge(out_of[b], len([1 for v in PLACE.values() if v[0] == b]))
            take_hi(0, 0, 16 * ((NPRE + 0) // 3 + 1))
            take_hi(1, 1, 16 * ((NPRE + 1) // 3 + 1))
            b1_0 = entry(1, 0, 1)
            with act.If(b1_0 > 0):
                turned_hi(1, xhi, 0, 1)
                turned_hi(1, xhi, 1, 2)
            turned_hi(0, xhi, 0, 2)
            turned_hi(0, xhi, 1, 3)
            with act.Fori(0, n_items) as i:
                b1, n1 = entry(1, i, 1), entry(2, i, MAX_ITEMS)
                b1x, n1x = entry(1, i + 1, 1), entry(2, i + 1, MAX_ITEMS)
                ex = entry(0, i + 1, NE - 1)
                for j in range(2, 6):
                    act.wait_ge(slab_used, i * 6 + (j - 1))
                    take_hi(j, j, (i * 2 + ((NPRE + j) // 3 + 1)) * 16)
                    half = (j - 2) // 2
                    if j % 2 == 0:
                        with act.If(b1 > 0):
                            sigmoid(1, half, n1 * 2 + half + 1)
                        sigmoid(0, half, i * 2 + half + 1)
                    else:
                        with act.If(b1 > 0):
                            turned_hi(1, hhi, half, n1 * 4 + 3 + half)
                        turned_hi(0, hhi, half, i * 5 + 5 + half)
                biases(ex, i * 2 + 2, n1x * 2)
                with act.If(b1x > 0):
                    turned_hi(1, xhi, 0, n1x * 4 + 1)
                    turned_hi(1, xhi, 1, n1x * 4 + 2)
                turned_hi(0, xhi, 0, i * 5 + 7)
                turned_hi(0, xhi, 1, i * 5 + 8)
                for s in range(2):
                    act.wait_ge(slab_used, i * 6 + 5 + s)
                    act.sem_inc(act_passed, 1)
                    with act.If(i + 1 < n_items):
                        take_hi(s, s, (i * 2 + ((NPRE + 6 + s) // 3 + 1)) * 16)
                    if s == 0:
                        act.wait_ge(gate_cp, i + 1)
                        act.wait_ge(idx_kept, i + 1)
                        act.sem_inc(act_passed, 1)
                    with act.If(b1 > 0):
                        act.wait_ge(y_full1, n1 * 2 + s + 1)
                        y_out(1, s)
                    y_out(0, s)
            act.wait_ge(all_added, 1)
            act.dma_start(lnq[:, 0, :], a["ln2_g"].partition_broadcast(P)).then_inc(lnq_in, 16)
            act.dma_start(lnq[:, 1, :], a["ln2_b"].partition_broadcast(P)).then_inc(lnq_in, 16)
            for t in range(NT):
                act.wait_ge(f_var, t + 1)
                act.activation(frs[:, 0, t:t + 1], fmv[:, t, 1:2], ACT.Sqrt, bias=consts[:, C_COL + 1:C_COL + 2])\
                   .then_inc(f_root, 1)
                act.wait_ge(f_sb, t + 1)
                act.activation(fin[:, t, :], fin[:, t, :], ACT.Identity, scale=frs[:, 0, t:t + 1],
                               bias=frs[:, 1, t:t + 1]).then_inc(f_norm, 1)

        @block.vector
        def _(dve):
            def heads(ap, width):
                return ap.unsqueeze(2).to_broadcast([P, 4, width])

            dve.wait_ge(consts_in, 32)
            dve.wait_ge(bias_in, 16)
            for j in range(4):
                b = filled(dve, ("small", j))
                frees(dve.tensor_copy(sm[:, 2 * j:2 * j + 2, :], b[:, 0:2 * SMALL].rearrange("p (t c) -> p t c", t=2)),
                      ("small", j))
            for j in range(4):
                copied(dve, ("small", j))
            for k in range(2):
                dve.tensor_tensor(gates_in[:, k, :].rearrange("p (h c) -> p h c", h=4),
                                  sm[:, :, R + 8 + 4 * k:R + 12 + 4 * k].rearrange("p c h -> p h c"),
                                  small_b[:, 4 * k:4 * k + 4].unsqueeze(2).to_broadcast([P, 4, NT]), ALU.add).then_inc(lf_in, 1)
            dve.wait_ge(lf_in, 2)
            dve.scalar_tensor_tensor(out=gates_in[:, 2, :], in0=gates_in[:, 1, :], scalar=-1.0, in1=gates_in[:, 1, :],
                                     op0=ALU.mult, op1=ALU.min).then_inc(lf_in, 1)
            for t in range(NT):
                dve.tensor_tensor_reduce(cT[:, t * P:(t + 1) * P], sm[:, t, 0:R], sm[:, t, 0:R], 1.0, 0.0,
                                         ALU.mult, ALU.add, rms_tmp[:, 0, t:t + 1]).then_inc(rms_sum, 1)
            dve.wait_ge(lf_ln, 1)
            dve.scalar_tensor_tensor(out=gates_in[:, 2, :], in0=gates_in[:, 1, :], scalar=0.0, in1=gates_in[:, 2, :],
                                     op0=ALU.min, op1=ALU.subtract).then_inc(lf_done, 1)
            dve.wait_ge(rms_root, 1)
            rstep = serial(dve, rms_step)
            rstep(dve.reciprocal(rms_tmp[:, 2, :], rms_tmp[:, 1, :]))
            dve.tensor_tensor(sm[:, :, 0:R], sm[:, :, 0:R], rms_tmp[:, 2, :].unsqueeze(2).to_broadcast([P, NT, R]),
                              ALU.mult).then_inc(rms_done, 1)
            r = 0
            for t in range(2, NT):
                sc = score_of(t)
                for h in range(AH):
                    for c in range(len(chunks(t))):
                        copied(dve, ("sc", t, h, c))
                    w = sm[:, t, R + h:R + h + 1]
                    if h:
                        dve.wait_ge(score_acc, r)
                        dve.scalar_tensor_tensor(out=sc, in0=rel[:, r % 2, 0:P * (t + 1)], scalar=w, in1=sc,
                                                 op0=ALU.mult, op1=ALU.add).then_inc(score_acc, 1)
                    else:
                        dve.tensor_scalar(sc, rel[:, r % 2, 0:P * (t + 1)], w, None, ALU.mult).then_inc(score_acc, 1)
                    r += 1
            gstep = serial(dve, gate_step)
            b = filled(dve, ("grow",))
            gstep(dve.tensor_copy(g_li[:, :], b[0:32, 0:P]))
            frees(dve.tensor_copy(g_e1[:, :], b[0:32, P:2 * P]), ("grow",))
            copied(dve, ("grow",))
            gstep(dve.tensor_tensor_scan(g_b[:, :], onesf[0:32, :], g_e1[:, :], 0.0, ALU.mult, ALU.add))
            gstep(dve.tensor_tensor(g_r[:, :], g_li[:, :], g_b[:, :], ALU.subtract))
            dve.tensor_tensor_scan(g_tmp[:, :], g_r[:, :], g_r[:, :], -3.0e38, ALU.max, ALU.max).then_inc(rows_done, 1)
            b = filled(dve, ("grow2",))
            frees(dve.tensor_copy(g_rowbuf[:, 0:2, :].rearrange("p a b -> p (a b)"), b[0:1, 0:64]), ("grow2",))
            copied(dve, ("grow2",))
            for h in range(MH):
                s = slice(h * 8, h * 8 + 8)
                gstep(dve.tensor_tensor_scan(g_rowbuf[:, 2, s], g_rowbuf[:, 1, s], g_rowbuf[:, 0, s], -1e30,
                                             ALU.max, ALU.add))
            gstep(dve.memset(g_rowbuf[:, 3, :], -1e30))
            dve.tensor_copy(g_rowbuf[:, 3, :].rearrange("p (h c) -> p h c", h=4)[:, :, 1:8],
                            g_rowbuf[:, 2, :].rearrange("p (h c) -> p h c", h=4)[:, :, 0:7]).then_inc(mrow_done, 1)
            b = filled(dve, ("mprev",))
            frees(dve.tensor_copy(g_col[:, 0:1], b[0:32, 0:1]), ("mprev",))
            copied(dve, ("mprev",))
            gstep(dve.tensor_scalar(g_g[:, :], g_tmp[:, :], g_col[:, 0:1], None, ALU.max))
            gstep(dve.tensor_scalar(g_ng[:, :], g_g[:, :], -1.0, None, ALU.mult))
            dve.tensor_tensor(g_tmp[:, :], g_b[:, :], g_g[:, :], ALU.add).then_inc(g_done, 1)
            dve.wait_ge(gexp_done, 1)
            dve.tensor_scalar(g_diag[:, :], ident[0:32, 0:32], g_col[:, 1:2], None, ALU.mult).then_inc(diag_done, 1)
            b = filled(dve, ("gcol",))
            frees(dve.tensor_copy(gate_cols[:, :, :].rearrange("p a b -> p (a b)"), b[:, 0:160]), ("gcol",))
            copied(dve, ("gcol",))

            tstep = serial(dve, topk_step)

            def selection():
                for t in range(NT):
                    sc, n = score_of(t), P * (t + 1)
                    if t < 2:
                        tstep(dve.tensor_copy(sc, dist_of(t)))
                        tstep(dve.memset(sc[0:64, n - 64:n], FAR))
                        continue
                    tstep(dve.memset(sc[0:64, n - 64:n], OUTSIDE))
                    for _ in range(TOPK // 8):
                        tstep(dve.max(top8[:, :], sc))
                        tstep(dve.match_replace(sc, top8[:, :], sc, PICKED))
                        yield
                    tstep(dve.tensor_scalar(sc, sc, PICKED, FAR, ALU.not_equal, ALU.mult))
                    tstep(dve.tensor_tensor(sc, sc, dist_of(t), ALU.max))
                    yield

            rounds = selection()

            def select(n):
                for _ in range(n):
                    next(rounds, None)

            hstep = serial(dve, ml_step)
            for c in range(NT):
                select(6)
                b = filled(dve, ("R", c))
                frees(dve.tensor_tensor(ma[:, :, :], b[:, :].rearrange("p (h t) -> p h t", h=4),
                                        cmask.unsqueeze(1).to_broadcast([P, 4, P]), ALU.add), ("R", c))
                select(6)
                b = filled(dve, ("S", c))
                dve.wait_ge(gate_exp, 4 * (c + 1))
                frees(dve.tensor_tensor(ma[:, :, :], b[:, :].rearrange("p (h t) -> p h t", h=4), ma[:, :, :], ALU.mult),
                      ("S", c))
                select(6)
                for q in range(2):
                    b = filled(dve, ("I", c, q))
                    part = b[:, 0:258].rearrange("p (h d) -> p h d", h=2)
                    if c:
                        copied(dve, ("X", c, q))
                        frees(dve.tensor_tensor(mnum[:, 2 * q:2 * q + 2, :], part, mst[:, 2 * q:2 * q + 2, :], ALU.add),
                              ("I", c, q))
                    else:
                        frees(dve.tensor_copy(mnum[:, 2 * q:2 * q + 2, :], part), ("I", c, q))
                for q in range(2 if c < NT - 1 else 0):
                    b = filled(dve, ("U", c, q))
                    part = b[:, 0:258].rearrange("p (h d) -> p h d", h=2)
                    if c:
                        dve.wait_ge(c_decayed, c)
                        frees(dve.tensor_tensor(mC[:, 2 * q:2 * q + 2, :], mC[:, 2 * q:2 * q + 2, :], part, ALU.add),
                              ("U", c, q))
                    else:
                        frees(dve.tensor_copy(mC[:, 2 * q:2 * q + 2, :], part), ("U", c, q))
                for q in range(2):
                    copied(dve, ("I", c, q))
                hstep(dve.scalar_tensor_tensor(out=m_den[:, 0, :], in0=mnum[:, :, MD], scalar=-1.0, in1=mnum[:, :, MD],
                                               op0=ALU.mult, op1=ALU.max))
                hstep(dve.tensor_tensor(m_den[:, 0, :], m_den[:, 0, :], gate_at(2, c), ALU.max))
                hstep(dve.reciprocal(m_den[:, 1, :], m_den[:, 0, :]))
                if c < NT - 1:
                    dve.wait_ge(wv_done, c + 1)
                hstep(dve.tensor_tensor(vaug[:, c, :, 0:MD], mnum[:, :, 0:MD], heads(m_den[:, 1, :], MD), ALU.mult))
                for h in range(MH):
                    dve.bn_stats(m_stat[:, h, :], vaug[:, c, h, 0:MD]).then_inc(h_written, 1)
                dve.wait_ge(h_written, 8 * c + 4)
                for h in range(MH):
                    dve.bn_aggr(m_mv[:, c, h, :], m_stat[:, h, :]).then_inc(h_written, 1)
                dve.wait_ge(h_written, 8 * c + 8)
            dve.tensor_scalar(m_rstd[:, :, :], m_mv[:, :, :, 1], EPS, None, ALU.add).then_inc(mvar_done, 1)
            select(6)
            dve.wait_ge(mroot, 1)
            dve.reciprocal(m_rstd[:, :, :], m_rstd[:, :, :]).then_inc(mnorm_in, 1)
            dve.wait_ge(mnorm_in, 1)
            dve.scalar_tensor_tensor(out=m_nmr[:, :, :], in0=m_mv[:, :, :, 0], scalar=-1.0, in1=m_rstd[:, :, :],
                                     op0=ALU.mult, op1=ALU.mult).then_inc(mnorm_in, 1)
            for _ in rounds:
                pass
            astep = serial(dve, att_step)
            for n in range(NT * AH + 4):
                if n < NT * AH:
                    t, h = divmod(n, AH)
                    ks = chunks(t)
                    for c, (k0, k1) in enumerate(ks):
                        b = filled(dve, ("L", n, c))
                        frees(dve.tensor_tensor_reduce(Lp[:, n % 3, k0:k1], b[:, 0:k1 - k0], score_of(t)[:, k0:k1], 1.0,
                                                       -3.0e38, ALU.subtract, ALU.max, att_m[:, n % 3, c:c + 1]),
                              ("L", n, c))
                    for c in range(len(ks)):
                        copied(dve, ("L", n, c))
                    dve.tensor_scalar(att_bias[:, n % 3:n % 3 + 1], att_m[:, n % 3, 0:1],
                                      att_m[:, n % 3, len(ks) - 1:len(ks)], -(2.0 ** -(h + 1)), ALU.max, ALU.mult)\
                       .then_inc(att_shift, 1)
                if 1 <= n <= NT * AH:
                    for g, (j0, j1) in list(enumerate(groups((n - 1) // AH)))[1:]:
                        b = filled(dve, ("T", n - 1, g))
                        frees(dve.tensor_copy(pT[:, (n - 1) % 2, j0:j1, :],
                                              b[:, 0:(j1 - j0) * P].rearrange("p (j q) -> p j q", q=P)), ("T", n - 1, g))
                if n >= 9 and n % AH == 1:
                    t = n // AH - 1
                    dve.wait_ge(o_full, t + 1)
                    dve.wait_ge(p_ready, AH * (t + 1))
                    astep(dve.reciprocal(att_rec[:, :], att_sum[:, t % 2, :]))
                    if t:
                        filled(dve, ("at", t - 1))
                    dve.tensor_tensor(ao[:, :].rearrange("p (h d) -> p h d", h=AH),
                                      ps[NB][:, :].rearrange("p (h d) -> p h d", h=AH),
                                      att_rec[:, :].unsqueeze(2).to_broadcast([P, AH, AD]), ALU.mult).then_inc(o_copied, 1)
            lstep = serial(dve, ln_step)

            def ln1_finish(t):
                dve.wait_ge(ln_root, t + 1)
                lstep(dve.reciprocal(ln_rstd[:, t % 2, 0:1], ln_rstd[:, t % 2, 0:1]))
                dve.scalar_tensor_tensor(out=ln_rstd[:, t % 2, 1:2], in0=ln_mv[:, t % 2, 0:1], scalar=-1.0,
                                         in1=ln_rstd[:, t % 2, 0:1], op0=ALU.mult, op1=ALU.mult).then_inc(ln_sb, 1)

            def ln1_affine(t):
                dve.wait_ge(ln_norm, t + 1)
                lstep(dve.tensor_tensor(h1all[:, t, :], h1all[:, t, :], lnp[:, 0, :], ALU.mult))
                dve.tensor_tensor(h1all[:, t, :], h1all[:, t, :], lnp[:, 1, :], ALU.add).then_inc(h1_done, 1)

            def router_top(t):
                b = filled(dve, ("rtt", t))
                frees(dve.tensor_tensor(lg[:, t, :], b[:, 0:NE], br[:, :], ALU.add), ("rtt", t))
                copied(dve, ("rtt", t))
                lstep(dve.max(top_v[:, t, :], lg[:, t, :]))
                lstep(dve.max_index(top_i[:, t, :], top_v[:, t, :], lg[:, t, :]))

            dve.wait_ge(xres_in, 64)
            dve.wait_ge(lnp_in, 80)
            for t in range(NT):
                for n in range(2):
                    b = filled(dve, ("mix", t, n))
                    half = h1all[:, t, n * 512:(n + 1) * 512]
                    frees(dve.scalar_tensor_tensor(out=half, in0=half, scalar=ALPHA, in1=b[:, :],
                                                   op0=ALU.mult, op1=ALU.add), ("mix", t, n))
                for n in range(2):
                    copied(dve, ("mix", t, n))
                    lstep(dve.bn_stats(ln_stat[:, t % 2, n, :], h1all[:, t, n * 512:(n + 1) * 512]))
                dve.bn_aggr(ln_mv[:, t % 2, :], ln_stat[:, t % 2, :, :].rearrange("p a b -> p (a b)")).then_inc(ln_var, 1)
                dve.wait_ge(ln_var, t + 1)
                ln1_finish(t)
                ln1_affine(t)
                if t > 1:
                    router_top(t - 2)
            router_top(NT - 2)
            router_top(NT - 1)
            rs = serial(dve, rt_step)
            rs(dve.tensor_copy(idxf[:, :, :], top_i[:, :, 0:4]))
            dve.tensor_tensor(gexp[:, :, :], top_v[:, :, 0:4], top_v[:, :, 0:1].to_broadcast([P, NT, 4]),
                              ALU.subtract).then_inc(rt_diff, 1)
            k_inner = hot[:, :, :, :].rearrange("p t k e -> p t e k")
            iota_tk = iota_e.unsqueeze(1).to_broadcast([P, 4, NE])
            for t in range(NT):
                rs(dve.tensor_tensor(hot[:, t, :, :], iota_tk, idxf[:, t, :].unsqueeze(2).to_broadcast([P, 4, NE]),
                                     ALU.is_equal))
            rs(dve.tensor_reduce(picks[:, :, :], k_inner, AX.X, ALU.add))
            dve.tensor_copy(picks_b[:, :, :], picks[:, :, :]).then_inc(picks_done, 1)
            dve.wait_ge(rt_exp, 1)
            rs(dve.tensor_reduce(gsum[:, 0, :], gexp[:, :, :], AX.X, ALU.add))
            rs(dve.reciprocal(gsum[:, 1, :], gsum[:, 0, :]))
            rs(dve.tensor_tensor(gexp[:, :, :], gexp[:, :, :], gsum[:, 1, :].unsqueeze(2).to_broadcast([P, NT, 4]), ALU.mult))
            for t in range(NT):
                rs(dve.tensor_tensor(hot[:, t, :, :], hot[:, t, :, :], gexp[:, t, :].unsqueeze(2).to_broadcast([P, 4, NE]),
                                     ALU.mult))
            dve.tensor_reduce(gates[:, :, :], k_inner, AX.X, ALU.add).then_inc(gates_done, 1)
            b = filled(dve, ("cnt",))
            rs(dve.tensor_copy(tot[:, :, :].rearrange("p t e -> p (t e)"), b[:, 0:256]))
            rs(dve.memset(base[:, 0, :], 0.0))
            for t in range(1, NT):
                rs(dve.tensor_tensor(base[:, t, :], base[:, t - 1, :], tot[:, t - 1, :], ALU.add))
            count, n_of, ends, first, near, aux = (rt_t[:, k, :] for k in range(6))
            rs(dve.tensor_tensor(count, base[:, NT - 1, :], tot[:, NT - 1, :], ALU.add))
            rs(dve.tensor_scalar(n_of, count, float(CAP), 1.0, ALU.is_gt, ALU.add))
            for k in range(2, S // CAP):
                rs(dve.scalar_tensor_tensor(out=n_of, in0=count, scalar=float(CAP * k), in1=n_of, op0=ALU.is_gt, op1=ALU.add))
            rs(dve.tensor_tensor_scan(ends, onesf[:, 0:NE], n_of, 0.0, ALU.mult, ALU.add))
            rs(dve.tensor_tensor(first, ends, n_of, ALU.subtract))
            rs(dve.tensor_scalar(near, first, float(CAP), None, ALU.mult))
            rs(dve.tensor_tensor(gslot[:, :, :].rearrange("p t e -> p (t e)"), base[:, :, :].rearrange("p t e -> p (t e)"),
                                 b[:, 256:512], ALU.add))
            rs(dve.tensor_tensor(gslot[:, :, :], gslot[:, :, :], near.unsqueeze(1).to_broadcast([P, NT, NE]), ALU.add))
            rs(dve.tensor_scalar(gslot[:, :, :], gslot[:, :, :], 1.0e6, None, ALU.add))
            rs(dve.tensor_tensor(gslot[:, :, :], gslot[:, :, :], picks[:, :, :], ALU.mult))
            frees(dve.tensor_scalar(gslot[:, :, :], gslot[:, :, :], -1.0e6, None, ALU.add), ("cnt",))
            item = consts[:, C_COL:C_COL + 1]
            rs(dve.tensor_scalar(near, ends, item, None, ALU.is_le))
            rs(dve.tensor_reduce(rt_c[:, 2:3], near, AX.X, ALU.add))
            rs(dve.tensor_scalar(rt_c[:, 0:1], rt_c[:, 2:3], float(NE - 1), None, ALU.min))
            rs(dve.tensor_tensor(aux, near, n_of, ALU.mult))
            rs(dve.tensor_reduce(rt_c[:, 3:4], aux, AX.X, ALU.add))
            rs(dve.tensor_scalar(near, iota_e, rt_c[:, 0:1], None, ALU.is_equal))
            rs(dve.tensor_tensor(aux, near, count, ALU.mult))
            rs(dve.tensor_reduce(rt_c[:, 4:5], aux, AX.X, ALU.add))
            rs(dve.tensor_tensor(rt_c[:, 5:6], rt_c[:, 3:4], item, ALU.subtract))
            rs(dve.scalar_tensor_tensor(out=rt_c[:, 6:7], in0=rt_c[:, 5:6], scalar=float(CAP), in1=rt_c[:, 4:5],
                                        op0=ALU.mult, op1=ALU.add))
            rs(dve.tensor_scalar(rt_c[:, 7:8], rt_c[:, 6:7], float(P), None, ALU.is_gt))
            rs(dve.tensor_scalar(rt_c[:, 8:9], ends[:, NE - 1:NE], item, None, ALU.is_gt))
            dve.tensor_tensor(rt_c[:, 1:2], rt_c[:, 7:8], rt_c[:, 8:9], ALU.mult).then_inc(items_done, 1)
            b = filled(dve, ("items",))
            rs(dve.tensor_copy(rt_row[:, 0, :], b[0:1, 0:MAX_ITEMS]))
            frees(dve.tensor_copy(rt_row[:, 1, :], b[0:1, P:P + MAX_ITEMS]), ("items",))
            copied(dve, ("items",))
            rs(dve.tensor_tensor_scan(rt_row[:, 3, :], onesf[0:1, 0:MAX_ITEMS], rt_row[:, 1, :], 0.0, ALU.mult, ALU.add))
            rs(dve.tensor_tensor(rt_row[:, 2, :], rt_row[:, 3, :], rt_row[:, 1, :], ALU.subtract))
            rs(dve.memset(rt_row[:, 3, :], 0.0))
            rs(dve.tensor_copy(rt_row[:, 3, 0:1], ends[0:1, NE - 1:NE]))
            dve.tensor_copy(table[:, :], rt_row[:, :, :].rearrange("p a b -> p (a b)")).then_inc(table_done, 1)
            for t in range(NT):
                if t >= 2:
                    dve.wait_ge(acc_out[t % 2], 16 * (t // 2))
                for n in range(2):
                    b = filled(dve, ("bd", t, n))
                    frees(dve.scalar_tensor_tensor(out=accst[:, t % 2, n * 512:(n + 1) * 512],
                                                   in0=h1all[:, t, n * 512:(n + 1) * 512], scalar=ALPHA, in1=b[:, :],
                                                   op0=ALU.mult, op1=ALU.add), ("bd", t, n))
                    copied(dve, ("bd", t, n))
                dve.sem_inc(acc_half, 1)

            entry = item_table(dve)
            dve.wait_ge(table_done, 1)
            n_items = dve.value_load(table[0:1, 3 * MAX_ITEMS:3 * MAX_ITEMS + 1], min_val=NE, max_val=MAX_ITEMS)

            def mark_slots(e, item, count):
                dve.tensor_scalar(relv[:, :], gslot[:, :, bass.ds(e, 1)].rearrange("p t o -> p (t o)"),
                                  consts[:, bass.ds(item + C_BASE, 1)], None, ALU.subtract).then_inc(rel_done, 1)
                dve.wait_ge(rel_done, count)
                dve.tensor_tensor(slots[:, :, :], consts[:, C_IOTA:C_IOTA + CAP].unsqueeze(1).to_broadcast([P, NT, CAP]),
                                  relv[:, :].unsqueeze(2).to_broadcast([P, NT, CAP]), ALU.is_equal).then_inc(slots_done, 1)

            def find_index(fill, steps, kept):
                dve.wait_ge(tr_full[0], since(fill))
                dve.tensor_copy(slot_n[:, :, :], ps[4][:, 0:8].rearrange("p (b k) -> p b k", b=2)[:, :, 0:3])\
                   .then_inc(tr_free[0], 1)
                dve.wait_ge(tr_free[0], since(fill))
                dve.scalar_tensor_tensor(out=slot_a[:, 0, :], in0=slot_n[:, :, 1], scalar=float(P), in1=slot_n[:, :, 0],
                                         op0=ALU.mult, op1=ALU.add).then_inc(idx_step, 1)
                dve.tensor_scalar(slot_a[:, 1, :], slot_n[:, :, 2], -4096.0, 4096.0, ALU.mult, ALU.add).then_inc(idx_step, 1)
                dve.wait_ge(idx_step, steps)
                dve.wait_ge(idx_kept, kept)
                dve.tensor_tensor(idx_next[:, :], slot_a[:, 0, :], slot_a[:, 1, :], ALU.add).then_inc(idx_done, 1)

            def take_lo(j, hi_count):
                for g in range(4):
                    dve.wait_ge(hi_done, hi_count + g)
                    s = slice(2 * g, 2 * g + 2)
                    dve.tensor_tensor(wlo[:, j % 2, s, :], raw[:, (j + 2) % 3, s, :], whi[:, j % 2, s, :].bitcast(f32),
                                      ALU.subtract).then_inc(lo_done if g == 3 else lo_part, 1)

            def turned_lo(b, hi_buf, lo_buf, g, count):
                dve.wait_ge(tr_hi[b], count)
                s = (slice(None), slice(4 * g, 4 * g + 4), slice(b * P, (b + 1) * P))
                dve.tensor_tensor(lo_buf[s], ps[4 + b][:, :].rearrange("p (k q) -> p k q", q=P), hi_buf[s].bitcast(f32),
                                  ALU.subtract).then_inc(tr_free[b], 1)

            def add_biases(b, half, count):
                if b:
                    dve.wait_ge(gu_full1, count * 2 + 2)
                dve.wait_ge(hb_done[b], since(count))
                for k in range(2):
                    dve.tensor_tensor(gu[:, b, k, :], ps[2 * b + k][:, :],
                                      bgu[:, k * D + half * SLAB:k * D + (half + 1) * SLAB], ALU.add)\
                       .then_inc((g_read, u_read)[k][b], 1)

            starts(dve, g_read + u_read + tr_free)
            for n in range(2):
                dve.wait_ge(acc_out[n], 8 * NT)
            dve.wait_ge(h_out, 16 * NT)
            dve.tensor_scalar(relv[:, :], gslot[:, :, 0], 0.0, None, ALU.subtract).then_inc(rel_done, 1)
            dve.wait_ge(rel_done, 1)
            dve.tensor_tensor(slots[:, :, :], consts[:, C_IOTA:C_IOTA + CAP].unsqueeze(1).to_broadcast([P, NT, CAP]),
                              relv[:, :].unsqueeze(2).to_broadcast([P, NT, CAP]), ALU.is_equal).then_inc(slots_done, 1)
            find_index(1, 2, 0)
            take_lo(0, 1)
            take_lo(1, 5)
            b1_0 = entry(1, 0, 1)
            with dve.If(b1_0 > 0):
                turned_lo(1, xhi, xlo, 0, 1)
                turned_lo(1, xhi, xlo, 1, 2)
            turned_lo(0, xhi, xlo, 0, 1)
            turned_lo(0, xhi, xlo, 1, 2)
            with dve.Fori(0, n_items) as i:
                b1, n1 = entry(1, i, 1), entry(2, i, MAX_ITEMS)
                b1x, n1x = entry(1, i + 1, 1), entry(2, i + 1, MAX_ITEMS)
                e, ex = entry(0, i, NE - 1), entry(0, i + 1, NE - 1)
                dve.wait_ge(y_done[0], since(i * 2))
                dve.wait_ge(y_done[1], since(n1 * 2))
                dve.wait_ge(tokens_in, i + 1)
                dve.tensor_copy(gcol[:, :], xg[:, :, bass.ds(e + D, 1)].rearrange("p b o -> p (b o)")).then_inc(gate_cp, 1)
                mark_slots(ex, i + 1, i + 2)
                for j in range(2, 6):
                    take_lo(j, i * 24 + (4 * j + 1))
                    half = (j - 2) // 2
                    if j == 2:
                        find_index(i * 5 + 4, i * 2 + 4, i + 1)
                    if j % 2 == 0:
                        with dve.If(b1 > 0):
                            dve.wait_ge(bgu_in, i * 16 + 16)
                            add_biases(1, half, n1 * 2 + half)
                        dve.wait_ge(bgu_in, i * 16 + 16)
                        dve.wait_ge(slab_used, i * 6 + 2 * half + 2)
                        add_biases(0, half, i * 2 + half)
                    else:
                        with dve.If(b1 > 0):
                            turned_lo(1, hhi, hlo, half, n1 * 4 + 3 + half)
                        turned_lo(0, hhi, hlo, half, i * 4 + 3 + half)
                with dve.If(b1x > 0):
                    turned_lo(1, xhi, xlo, 0, n1x * 4 + 1)
                    turned_lo(1, xhi, xlo, 1, n1x * 4 + 2)
                turned_lo(0, xhi, xlo, 0, i * 4 + 5)
                turned_lo(0, xhi, xlo, 1, i * 4 + 6)
                with dve.If(i + 1 < n_items):
                    take_lo(0, i * 24 + 25)
                    take_lo(1, i * 24 + 29)
            fs = serial(dve, f_step)
            dve.wait_ge(lnq_in, 32)
            for t in range(NT):
                dve.wait_ge(fin_in[t // 4], 16)
                for n in range(2):
                    fs(dve.bn_stats(fstat[:, t, n, :], fin[:, t, n * 512:(n + 1) * 512]))
                dve.bn_aggr(fmv[:, t, :], fstat[:, t, :, :].rearrange("p a b -> p (a b)")).then_inc(f_var, 1)
                dve.wait_ge(f_root, t + 1)
                fs(dve.reciprocal(frs[:, 0, t:t + 1], frs[:, 0, t:t + 1]))
                dve.scalar_tensor_tensor(out=frs[:, 1, t:t + 1], in0=fmv[:, t, 0:1], scalar=-1.0,
                                         in1=frs[:, 0, t:t + 1], op0=ALU.mult, op1=ALU.mult).then_inc(f_sb, 1)
                dve.wait_ge(f_norm, t + 1)
                fs(dve.tensor_tensor(fin[:, t, :], fin[:, t, :], lnq[:, 0, :], ALU.mult))
                dve.tensor_tensor(fin[:, t, :], fin[:, t, :], lnq[:, 1, :], ALU.add).then_inc(f_done, 1)

        @block.gpsimd
        def _(pool):
            pool.memset(vaug[:, :, :, MD:MD + 1], 1.0).then_inc(ones_set, 1)
            filled(pool, last_sc)
            pool.memset(uT[:, :, 0:3], 0.0).then_inc(pad_set, 1)
            pool.wait_ge(late_in, 32)
            pool.wait_ge(pad_set, 1)
            pool.wait_ge(score_acc, n_sc)
            cs = serial(pool, conv_step)
            for m in range(4):
                for n in range(2):
                    copied(pool, ("u", m, n))
                if m:
                    pool.wait_ge(conv_done, m)
                tap = ucT[:, m + 1, :] if m < 3 else uT[:, 0, 0:S]
                cs(pool.tensor_scalar(ucT[:, m, :], uT[:, m, 0:S], convw[:, m, 0:1], None, ALU.mult))
                for k in range(1, 4):
                    cs(pool.tensor_scalar(tap, uT[:, m, k:k + S], convw[:, m, k:k + 1], None, ALU.mult))
                    ins = pool.tensor_tensor(ucT[:, m, :], ucT[:, m, :], tap, ALU.add)
                    if k < 3:
                        cs(ins)
                ins.then_inc(conv_done, 1)
            pool.wait_ge(normg_in, 16)
            for t in range(NT):
                copied(pool, ("z", t))
                pool.tensor_tensor(zs[:, t, :, :].rearrange("p h d -> p (h d)"), zs[:, t, :, :].rearrange("p h d -> p (h d)"),
                                   normg[:, :], ALU.mult).then_inc(zgated, 1)
            for c in range(NT - 1):
                copied(pool, ("v", c))
                copied(pool, ("gcol",))
                if c:
                    filled(pool, ("U", c - 1, 1))
                pool.tensor_tensor(mwv[:, :, :], vaug[:, c, :, :], gate_at(3, c).unsqueeze(2).to_broadcast([P, 4, MD + 1]),
                                   ALU.mult).then_inc(wv_done, 1)
                if c:
                    filled(pool, ("X", c, 1))
                    pool.tensor_tensor(mC[:, :, :], mC[:, :, :], gate_at(4, c).unsqueeze(2).to_broadcast([P, 4, MD + 1]),
                                       ALU.mult).then_inc(c_decayed, 1)
            for c in range(NT):
                pool.wait_ge(mnormed, 4 * (c + 1))
                pool.wait_ge(zgated, NT)
                pool.tensor_tensor(zs[:, c, :, :], vaug[:, c, :, 0:MD], zs[:, c, :, :], ALU.mult).then_inc(mout, 1)
            for n in range(2):
                pool.wait_ge(acc_out[n], 8 * NT)
            pool.wait_ge(h_out, 16 * NT)
            pool.wait_ge(gate_out, 16)
            pool.memset(xg[:, :, :], 0.0).then_inc(xg_set, 1)
            pool.wait_ge(xg_set, 1)
            entry = item_table(pool)
            pool.wait_ge(table_done, 1)
            n_items = pool.value_load(table[0:1, 3 * MAX_ITEMS:3 * MAX_ITEMS + 1], min_val=NE, max_val=MAX_ITEMS)

            def fetch(b):
                pool.indirect_dma_start(xg[:, b, :], None, hext, bass.IndirectOffsetOnAxis(idx_next[:, b:b + 1], 0),
                                        bounds_check=S - 1, oob_is_err=False).then_inc(gathered[b], 16)

            def give(b):
                pool.indirect_dma_start(acc, bass.IndirectOffsetOnAxis(idx_cur[:, b:b + 1], 0), ysb[:, b, :], None,
                                        bounds_check=S - 1, oob_is_err=False, compute_op=ALU.add).then_inc(added[b], 16)

            def until(s, value):
                pool.wait_ge(s, value)
                pool.sem_inc(pool_passed, 1)

            def swiglu(b, half, c):
                g, u, h = gu[:, b, 0, :], gu[:, b, 1, :], hb[:, b, half * SLAB:(half + 1) * SLAB]
                until(g_read[b], since(c + 1))
                pool.tensor_scalar(g, g, LIMIT, -3.0e38, ALU.min, ALU.max).then_inc(clip_g[b], 1)
                until(u_read[b], since(c + 1))
                pool.tensor_scalar(u, u, LIMIT, -LIMIT, ALU.min, ALU.max).then_inc(clip_u[b], 1)
                until(clip_g[b], c + 1)
                until(clip_u[b], c + 1)
                pool.tensor_scalar(u, u, 1.0, 1.0, ALU.add, ALU.mult).then_inc(up_done[b], 1)
                until(up_done[b], c * 2 + 1)
                pool.tensor_tensor(u, u, g, ALU.mult).then_inc(up_done[b], 1)
                until(up_done[b], c * 2 + 2)
                until(sig_done[b], c + 1)
                pool.tensor_tensor(h, h, u, ALU.mult).then_inc(hb_done[b], 1)

            starts(pool, hb_done)
            pool.wait_ge(idx_done, 1)
            fetch(0)
            b1_0 = entry(1, 0, 1)
            with pool.If(b1_0 > 0):
                fetch(1)
            pool.wait_ge(gathered[0], 16)
            with pool.If(b1_0 > 0):
                pool.wait_ge(gathered[1], 16)
            pool.sem_inc(tokens_in, 1)
            pool.tensor_copy(idx_cur[:, :], idx_next[:, :]).then_inc(idx_kept, 1)
            with pool.Fori(0, n_items) as i:
                b1, n1 = entry(1, i, 1), entry(2, i, MAX_ITEMS)
                b1x, n1x = entry(1, i + 1, 1), entry(2, i + 1, MAX_ITEMS)
                until(idx_done, i + 2)
                until(gate_cp, i + 1)
                until(tr_full[0], since(i * 5 + 3))
                fetch(0)
                with pool.If(b1x > 0):
                    until(tr_full[1], since(n1 * 4 + b1 * 2))
                    fetch(1)
                for half in range(2):
                    with pool.If(b1 > 0):
                        swiglu(1, half, n1 * 2 + half)
                    swiglu(0, half, i * 2 + half)
                until(gathered[0], i * 16 + 32)
                with pool.If(b1x > 0):
                    until(gathered[1], n1x * 16 + 16)
                pool.sem_inc(tokens_in, 1)
                until(y_done[0], since(i * 2 + 2))
                give(0)
                with pool.If(b1 > 0):
                    until(y_done[1], since(n1 * 2 + 2))
                    give(1)
                    until(added[1], n1 * 16 + 16)
                until(added[0], i * 16 + 16)
                pool.tensor_copy(idx_cur[:, :], idx_next[:, :]).then_inc(idx_kept, 1)
            pool.sem_inc(all_added, 1)


def constants():
    import numpy as np
    c = np.zeros((P, C_END), np.float32)
    p = np.arange(P)[:, None]
    c[:, C_ID:C_ID + P] = np.eye(P)
    c[:, C_MASK:C_MASK + P] = np.where(p > np.arange(P)[None], -1e30, 0.0)
    c[:, C_DIST:C_DIST + S] = np.abs(p + (S - P) - np.arange(S)[None])
    c[:, C_IOTA:C_IOTA + CAP] = np.arange(CAP)[None]
    for m in range(4):
        for par in range(2):
            c[par * 64:par * 64 + 64, C_QS + m] = 2.0 ** (2 * m + par + 1) / 8.0
    c[:, C_BASE:C_BASE + MAX_ITEMS + 1] = CAP * np.arange(MAX_ITEMS + 1)[None]
    c[:, C_COL] = np.arange(P)
    c[:, C_COL + 1] = EPS
    c[:, C_ONE:C_ONE + P] = 1.0
    b = np.zeros((P, 2 * P + 24), np.float32)
    b[:, 0:P] = 1.0
    b[:, P:2 * P] = p < np.arange(P)[None]
    for t in range(NT):
        b[:, 2 * P + 3 * t] = np.arange(P)
        b[:, 2 * P + 3 * t + 1] = t
        b[:, 2 * P + 3 * t + 2] = 1.0
    return c, b.astype(mybir.dt.np(mybir.dt.bfloat16))


def kernel(**inputs):
    import numpy as np
    import concourse.bacc as bacc
    from concourse.bass_utils import run_bass_kernel_spmd

    v = {k: np.asarray(x) for k, x in inputs.items()}

    def slab(w):
        return np.ascontiguousarray(w.reshape(KT, P, -1).transpose(1, 0, 2))

    w = v["w_in"][0]
    sizes = (512, 128, 512, 64, 8, 512, 512, 512, 4, 4)
    ends = np.cumsum(sizes)
    q_a, ckv, q_i, k_i, w_i, u, vv, z, gi, gf = (w[:, e - s:e] for s, e in zip(sizes, ends))
    consts, cb = constants()
    arrays = {
        "xT": slab(np.ascontiguousarray(v["x"][0].T)),
        "x": np.ascontiguousarray(v["x"][0].reshape(NT, P, D).transpose(1, 0, 2)),
        "w_qi": slab(q_i),
        "w_ks": slab(np.concatenate([k_i, k_i, ckv, w_i, gi, gf], axis=1)),
        "w_qa": slab(q_a), "w_u": slab(u), "w_v": slab(vv), "w_z": slab(z),
        "w_out": np.stack([slab(v["w_out"][0][:, n * 512:(n + 1) * 512]) for n in range(2)]),
        "kv_norm_g": np.ascontiguousarray(v["kv_norm_g"].reshape(P, 1)),
        "w_ukv": np.ascontiguousarray(np.stack([v["w_uk"][0].transpose(1, 0, 2).reshape(P, 512),
                                                v["w_uv"][0].transpose(1, 0, 2).reshape(P, 512)], axis=1)),
        "conv": np.ascontiguousarray(np.concatenate([v["m_conv_w"][0], v["m_conv_b"]], axis=0)
                                     .reshape(5, 4, P).transpose(2, 1, 0)),
        "w_m": np.ascontiguousarray(np.stack([v["w_mq"][0], v["w_mk"][0]]).transpose(2, 0, 1, 3)),
        "b_if": np.concatenate([v["b_i"][0], v["b_f"][0]]),
        "m_norm_g": v["m_norm_g"][0],
        "ln1_g": v["ln1_g"][0], "ln1_b": v["ln1_b"][0], "ln2_g": v["ln2_g"][0], "ln2_b": v["ln2_b"][0],
        "w_router": slab(v["w_router"][0]), "b_router": v["b_router"][0],
        "w_gu": np.ascontiguousarray(v["w_gu"][0].reshape(NE, KT, P, 2, 2, SLAB).transpose(0, 4, 3, 2, 1, 5)
                                     .reshape(4 * NE, P, KT, SLAB)),
        "w_dn": np.ascontiguousarray(v["w_down"][0].reshape(NE, KT, P, 2, SLAB).transpose(0, 3, 2, 1, 4)
                                     .reshape(2 * NE, P, KT, SLAB)),
        "b_gu": v["b_gu"][0], "b_down": v["b_down"][0],
        "consts": consts, "cb": cb,
    }
    nc = bacc.Bacc("TRN2", target_bir_lowering=False, num_devices=1)
    aps = {k: nc.dram_tensor("in_" + k, x.shape, mybir.dt.from_np(x.dtype), kind="ExternalInput").ap()
           for k, x in arrays.items()}
    out = nc.dram_tensor("out", (1, S, D), mybir.dt.float32, kind="ExternalOutput").ap()
    layer_kernel(nc, aps, out)
    got = run_bass_kernel_spmd(nc, [{"in_" + k: x for k, x in arrays.items()}], core_ids=[0])
    return got.results[0]["out"]
```

```python
from contextlib import ExitStack

import concourse.bass as bass
from concourse import mybir

P = 128
D = 1024
S = 1024
NT = S // P
KT = D // P
SLAB = 512
AH, AD = 8, 64
R = 128
MH, MD = 4, 128
SMALL = R + 8 + 4 + 4
NE = 32
CAP = 2 * P
MAX_ITEMS = 64
TOPK = 256
PICKED = -1e30
OUTSIDE = -2e30
FAR = 1e30
EPS = 1e-5
ALPHA = 2.0 ** 0.25
LIMIT = 7.0
HROW = D + NE

C_ID, C_MASK, C_DIST, C_IOTA, C_QS, C_BASE, C_COL, C_ONE, C_END = (
    0, 128, 256, 1280, 1536, 1540, 1606, 1608, 1736)


def chunks(t):
    n = P * (t + 1)
    return [(a, min(a + SLAB, n)) for a in range(0, n, SLAB)]


def groups(t):
    return [(a, min(a + 4, t + 1)) for a in range(0, t + 1, 4)]


def task_order():
    o = [("qi", m, n) for n in range(2) for m in range(4)] + [("ki", n) for n in range(2)]
    o += [("small", j) for j in range(4)]
    o += [("sc", t, h, c) for t in range(2, NT) for h in range(AH) for c in range(len(chunks(t)))]
    o += [("grow",)]
    o += [("qa", m, n) for n in range(2) for m in range(4)]
    o += [("grow2",), ("mprev",)]
    o += [("u", m, n) for n in range(2) for m in range(4)]
    o += [("gcol",)]
    o += [("v", t) for t in range(NT)] + [("z", t) for t in range(NT)]
    o += [("ct", j) for j in range(2)]
    for c in range(NT):
        o += [("mq", c), ("mk", c), ("mkt", c), ("R", c), ("S", c)]
        o += [("X", c, q) for q in range(2) if c]
        o += [("I", c, q) for q in range(2)]
        o += [("U", c, q) for q in range(2) if c < NT - 1]
    o += [("mt", c) for c in range(NT)]
    o += [("kt", m, n) for n in range(2) for m in range(4)] + [("V", t) for t in range(NT)]
    for n in range(NT * AH + 4):
        if n < NT * AH:
            o += [("L", n, c) for c in range(len(chunks(n // AH)))]
        if 1 <= n <= NT * AH:
            o += [("T", n - 1, g) for g in range(len(groups((n - 1) // AH)))]
        if n >= 11 and n % AH == 3:
            o += [("at", n // AH - 1)]
    for t in range(NT):
        o += [("mix", t, 0), ("mix", t, 1)]
        if t:
            o += [("ht", t - 1, 0), ("ht", t - 1, 1)]
        if t > 1:
            o += [("rt", t - 2), ("rtt", t - 2)]
    o += [("ht", NT - 1, 0), ("ht", NT - 1, 1)]
    for t in (NT - 2, NT - 1):
        o += [("rt", t), ("rtt", t)]
    o += [("cnt",), ("items",)] + [("gt", j) for j in range(2)]
    o += [("bd", t, n) for t in range(NT) for n in range(2)]
    return o


NB = 7
ORDER = task_order()
PLACE = {task: (n % NB, n // NB) for n, task in enumerate(ORDER)}


def layer_kernel(nc, a, out):
    f32, f32r, bf16 = mybir.dt.float32, mybir.dt.float32r, mybir.dt.bfloat16
    i32, u32 = mybir.dt.int32, mybir.dt.uint32
    ALU, ACT, AX = mybir.AluOpType, mybir.ActivationFunctionType, mybir.AxisListType

    ctx = ExitStack()
    with ctx:
        KB = 1024
        LOW = 16512

        def at(name, kb, shape, dt=f32):
            return nc.alloc_sbuf_tensor_at(name, shape, dt, offset=LOW + int(kb * KB) // 32 * 32)

        def sem(name):
            return ctx.enter_context(nc.semaphore(name))

        raw = at("raw", 0, [P, 3, KT, SLAB])
        consts = at("consts", 48, [P, C_END])
        small_b = at("small_b", 54.8, [P, 8])
        gates_in = at("gates_in", 54.85, [P, 3, 32])
        g_li = at("g_li", 55.25, [32, P])
        g_b = at("g_b", 55.75, [32, P])
        g_r = at("g_r", 56.25, [32, P])
        g_g = at("g_g", 56.75, [32, P])
        g_ng = at("g_ng", 57.25, [32, P])
        g_e1 = at("g_e1", 57.75, [32, P])
        g_e2 = at("g_e2", 58.25, [32, P])
        g_w = at("g_w", 58.75, [32, P])
        g_tmp = at("g_tmp", 59.25, [32, P])
        g_rowbuf = at("g_rowbuf", 59.75, [1, 4, 32])
        g_col = at("g_col", 60.25, [32, 4])
        g_diag = at("g_diag", 60.375, [32, 32])
        gate_cols = at("gate_cols", 60.5, [P, 5, 32])
        rms_tmp = at("rms_tmp", 61.25, [P, 3, 8])
        att_m = at("att_m", 61.5, [P, 3, 4])
        att_bias = at("att_bias", 61.6, [P, 3])
        att_sum = at("att_sum", 61.65, [P, 2, 8])
        att_rec = at("att_rec", 61.75, [P, 8])
        top8 = at("top8", 61.8, [P, 8])
        m_stat = at("m_stat", 61.85, [P, 4, 6])
        m_mv = at("m_mv", 61.95, [P, NT, 4, 2])
        m_rstd = at("m_rstd", 62.25, [P, NT, 4])
        m_nmr = at("m_nmr", 62.4, [P, NT, 4])
        m_den = at("m_den", 62.6, [P, 2, 4])
        ln_stat = at("ln_stat", 62.65, [P, 2, 2, 6])
        ln_mv = at("ln_mv", 62.75, [P, 2, 2])
        ln_rstd = at("ln_rstd", 62.8, [P, 2, 2])
        X = 64
        xT = at("xT", X, [P, KT, S])
        catT = at("catT", X, [P, KT, S])
        qiT = at("qiT", X + 32, [P, 4, S])
        kiT = at("kiT", X + 48, [P, S])
        score = at("score", X + 52, [P, 36 * P])
        qaT = at("qaT", X + 70, [P, 4, S])
        ucT = at("ucT", X + 86, [P, 4, S])
        vaug = at("vaug", X + 102, [P, NT, 4, MD + 1])
        zs = at("zs", X + 118.5, [P, NT, 4, MD])
        Vn = at("Vn", X + 102, [P, NT, AH * AD])
        KTr = at("KTr", X + 118.5, [P, 4, S])
        sm = at("sm", X + 134.5, [P, NT, SMALL])
        cT = at("cT", X + 139.1, [P, S])
        rel = at("rel", X + 86, [P, 2, S])
        uT = at("uT", X + 32, [P, 4, S + 3])
        normg = at("normg", X + 48.5, [P, 512])
        convw = at("convw", 63.7, [P, 4, 5])
        g_kv = at("g_kv", 63.9, [P, 1])
        mqk = at("mqk", X + 32, [P, 3, 4, MD])
        ma = at("ma", X + 38, [P, 4, P])
        mwv = at("mwv", X + 40, [P, 4, MD + 1])
        mnum = at("mnum", X + 42.1, [P, 4, MD + 1])
        mst = at("mst", X + 44.2, [P, 4, MD + 1])
        mC = at("mC", X + 46.3, [P, 4, MD + 1])
        w_m = at("w_m", X + 66, [P, 2, 4, MD])
        Lp = at("Lp", X + 32, [P, 3, S])
        pT = at("pT", X + 44, [P, 2, NT, P])
        ao = at("ao", X + 134.5, [P, 512])
        w_ukv = at("w_ukv", X, [P, 2, 512])
        w_m = at("w_m", X + 4, [P, 2, 4, MD])
        h1all = at("h1all", X + 70, [P, NT, D])
        lnp = at("lnp", X + 32, [P, 2, D])
        h1T = at("h1T", X + 40, [P, 2, KT, P])
        bdown = at("bdown", X + 48, [NE, D])
        GT = at("GT", X + 52, [NE, S])
        accst = at("accst", X + 56, [P, 2, D])
        w_rt = at("w_rt", X + 64, [P, KT, NE])
        br = at("br", X + 65, [P, NE])
        lgT = at("lgT", X + 65.25, [NE, 2, P])
        lg = at("lg", X + 66.25, [P, NT, NE])
        top_v = at("top_v", X + 67.25, [P, NT, 8])
        top_i = at("top_i", X + 67.5, [P, NT, 8], u32)
        idxf = at("idxf", X + 67.75, [P, NT, 4])
        gexp = at("gexp", X + 68, [P, NT, 4])
        gsum = at("gsum", X + 68.25, [P, 2, NT])
        hot = at("hot", X + 134.5, [P, NT, 4, NE])
        rt_t = at("rt_t", X + 138.5, [P, 10, NE])
        rt_c = at("rt_c", X + 140, [P, 12])
        rt_row = at("rt_row", X + 140.5, [1, 4, MAX_ITEMS])
        gslot = at("gslot", 55.25, [P, NT, NE])
        gates = at("gates", 56.25, [P, NT, NE])
        picks = at("picks", 57.25, [P, NT, NE])
        tot = at("tot", 58.25, [P, NT, NE])
        base = at("base", 59.25, [P, NT, NE])
        picks_b = at("picks_b", 60.25, [P, NT, NE], bf16)
        table = at("table", 61, [1, 4 * MAX_ITEMS], i32)
        cb = at("cb", 63, [P, 2 * P + 24], bf16)
        whi = at("whi", X + 102, [P, 2, KT, SLAB], f32r)
        wlo = at("wlo", X, [P, 2, KT, SLAB], f32r)
        xhi = at("xhi", X + 32, [P, KT, CAP], f32r)
        xlo = at("xlo", X + 40, [P, KT, CAP], f32r)
        hhi = at("hhi", X + 48, [P, KT, CAP], f32r)
        hlo = at("hlo", X + 56, [P, KT, CAP], f32r)
        hb = at("hb", X + 64, [P, 2, D])
        xg = at("xg", X + 72, [P, 2, HROW])
        ysb = at("ysb", X + 80.5, [P, 2, D])
        slots = at("slots", X + 88.5, [P, NT, CAP], bf16)
        gu = at("gu", X + 92.5, [P, 2, 2, SLAB])
        bgu = at("bgu", X + 134.5, [P, 2 * D])
        relv = at("relv", 62, [P, NT])
        act_tmp = at("act_tmp", 62.6, [P, 1])
        slot_n = at("slot_n", 62.05, [P, 2, 3])
        slot_a = at("slot_a", 62.1, [P, 2, 2])
        idx_next = at("idx_next", 62.15, [P, 2], u32)
        idx_mid = at("idx_mid", 62.65, [P, 2], u32)
        idx_cur = at("idx_cur", 62.2, [P, 2], u32)
        gcol = at("gcol", 62.25, [P, 2])
        fin = at("fin", X + 102, [P, NT, D])
        lnq = at("lnq", X, [P, 2, D])
        fstat = at("fstat", X + 8, [P, NT, 2, 6])
        fmv = at("fmv", X + 9, [P, NT, 2])
        frs = at("frs", X + 9.25, [P, 2, NT])

        ps = [ctx.enter_context(nc.psum_tensor(f"ps{n}", [P, 512], f32)) for n in range(8)]
        hext = nc.dram_tensor("hext", [S, HROW], f32, kind="Internal").ap()
        acc = nc.dram_tensor("acc", [S, D], f32, kind="Internal").ap()

        ident = consts[:, C_ID:C_ID + P]
        cmask = consts[:, C_MASK:C_MASK + P]
        onesf = consts[:, C_ONE:C_ONE + P]
        iota_e = consts[:, C_IOTA:C_IOTA + NE]
        slab_slot = lambda q: q % 3

        def score_of(t):
            o = P * t * (t + 1) // 2
            return score[:, o:o + P * (t + 1)]

        def dist_of(t):
            return consts[:, C_DIST + S - P * (t + 1):C_DIST + S]

        def gate_at(k, c):
            return gate_cols[:, k, :].rearrange("p (h c) -> p h c", h=4)[:, :, c]

        full = [sem(f"bank_full{n}") for n in range(NB)]
        out_of = [sem(f"bank_copied{n}") for n in range(NB)]

        def bank(task):
            return ps[PLACE[task][0]]

        def filled(eng, task):
            b, u = PLACE[task]
            eng.wait_ge(full[b], u + 1)
            return ps[b]

        def copied(eng, task):
            b, u = PLACE[task]
            eng.wait_ge(out_of[b], u + 1)

        def frees(ins, task):
            ins.then_inc(out_of[PLACE[task][0]], 1)

        def serial(eng, s):
            n = [0]

            def step(ins):
                ins.then_inc(s, 1)
                n[0] += 1
                eng.wait_ge(s, n[0])
            return step

        x_in = [sem(f"x_in{n}") for n in range(2)]
        raw_in = [sem(f"raw_in{n}") for n in range(3)]
        consts_in, bias_in, wm_in, late_in, normg_in = (
            sem("consts_in"), sem("bias_in"), sem("wm_in"), sem("late_in"), sem("normg_in"))
        xres_in, lnp_in, lnq_in = sem("xres_in"), sem("lnp_in"), sem("lnq_in")
        score_acc, gates_cp = sem("score_acc"), sem("gates_cp")
        topk_step, gate_step, rms_step, ml_step = sem("topk_step"), sem("gate_step"), sem("rms_step"), sem("ml_step")
        lf_in, lf_exp, lf_ln, lf_done = sem("lf_in"), sem("lf_exp"), sem("lf_ln"), sem("lf_done")
        rows_done, mrow_done, g_done, gexp_step, gexp_done, diag_done = (
            sem("rows_done"), sem("mrow_done"), sem("g_done"), sem("gexp_step"), sem("gexp_done"), sem("diag_done"))
        rms_sum, rms_root, rms_done = sem("rms_sum"), sem("rms_root"), sem("rms_done")
        pad_set, conv_step, conv_done, uc_ready = sem("pad_set"), sem("conv_step"), sem("conv_done"), sem("uc_ready")
        ones_set, zgated = sem("ones_set"), sem("zgated")
        gate_exp, wv_done, c_decayed, x_part, h_written = (
            sem("gate_exp"), sem("wv_done"), sem("c_decayed"), sem("x_part"), sem("h_written"))
        mvar_done, mroot, mnorm_in, mnormed, mout = (
            sem("mvar_done"), sem("mroot"), sem("mnorm_in"), sem("mnormed"), sem("mout"))
        att_shift, p_ready, o_full, o_copied, att_step = (
            sem("att_shift"), sem("p_ready"), sem("o_full"), sem("o_copied"), sem("att_step"))
        ln_step, ln_var, ln_root, ln_sb, ln_norm, h1_done = (
            sem("ln_step"), sem("ln_var"), sem("ln_root"), sem("ln_sb"), sem("ln_norm"), sem("h1_done"))
        rt_step, rt_diff, rt_exp, picks_done, items_done, table_done = (
            sem("rt_step"), sem("rt_diff"), sem("rt_exp"), sem("picks_done"), sem("items_done"), sem("table_done"))
        gates_done, acc_half, h_out, acc_out, gate_out = (
            sem("gates_done"), sem("acc_half"), sem("h_out"), [sem(f"acc_out{n}") for n in range(2)], sem("gate_out"))
        hi_done, lo_done, piece_used = sem("hi_done"), sem("lo_done"), sem("piece_used")
        lo3_done = sem("lo3_done")
        rest_in = [sem(f"rest_in{n}") for n in range(3)]
        gu_full1 = sem("gu_full1")
        gu_read = [sem(f"gu_read{n}") for n in range(2)]
        sig_done = [sem(f"sig_done{b}") for b in range(2)]
        clip_g = [sem(f"clip_g{b}") for b in range(2)]
        clip_u = [sem(f"clip_u{b}") for b in range(2)]
        up_done = [sem(f"up_done{b}") for b in range(2)]
        hb_done = [sem(f"hb_done{b}") for b in range(2)]
        tr_full = [sem(f"tr_full{n}") for n in range(2)]
        tr_hi = [sem(f"tr_hi{n}") for n in range(2)]
        tr_free = [sem(f"tr_free{n}") for n in range(2)]
        y_full1 = sem("y_full1")
        y_done = [sem(f"y_done{b}") for b in range(2)]
        gathered = [sem(f"gathered{b}") for b in range(2)]
        added = [sem(f"added{b}") for b in range(2)]
        gate_cp, idx_step, idx_done, slots_done, rel_done, idx_kept, bgu_in = (
            sem("gate_cp"), sem("idx_step"), sem("idx_done"), sem("slots_done"), sem("rel_done"),
            sem("idx_kept"), sem("bgu_in"))
        act_table = sem("act_table")
        sum_kept = sem("sum_kept")
        tokens_in = sem("tokens_in")
        pool_passed, sp_passed = sem("pool_passed"), sem("sp_passed")
        xg_set, all_added = sem("xg_set"), sem("all_added")
        fin_in, f_step, f_var, f_root, f_sb, f_norm, f_done, f_out = (
            [sem(f"fin_in{n}") for n in range(2)], sem("f_step"), sem("f_var"), sem("f_root"), sem("f_sb"), sem("f_norm"),
            sem("f_done"), sem("f_out"))

        last_use = [("qi", 3, 1), ("small", 3), ("qa", 3, 1), ("u", 3, 1), ("v", NT - 1), ("z", NT - 1),
                    ("mix", NT - 1, 0), ("mix", NT - 1, 1)]
        last_sc = ("sc", NT - 1, AH - 1, 1)
        NPRE = len(last_use)
        n_sc = (NT - 2) * AH

        def item_table(eng):
            def entry(row, i, top):
                return eng.value_load(table[0:1, bass.ds(i + row * MAX_ITEMS, 1)], min_val=0, max_val=top)
            return entry

        def since(n, more=0):
            return n + (more + 2)

        def starts(eng, sems):
            for s in sems:
                eng.sem_inc(s, 2)

        Y_BANK = ((6, 7), (3, 5))
        TR_BANK = (2, 4)

        def gu_place(b, quarter, i, n1, blocks):
            if len(blocks) == 2:
                return 1 - b, i * 2 + n1 * 2 + quarter
            return quarter % 2, i * 2 + n1 * 2 + quarter // 2

        def piece_split(eng, i, j, g):
            if g < 3:
                eng.wait_ge(lo_done, i * 18 + (3 * j + g + 1))
            else:
                eng.wait_ge(lo3_done, i * 6 + (j + 1))

        SLOTS = 1

        def fill_of(i, what, n, slots=SLOTS):
            place = {("h", 0): slots + 1, ("h", 2): slots + 2, ("x", 0): slots + 3, ("x", 2): slots + 4,
                     ("h", 1): 1, ("x", 1): 2, ("h", 3): 3, ("x", 3): 4}[what, n]
            if n % 2 == 0:
                return i * (4 + slots) + (2 + slots + place)
            return i * 4 + (2 + place)

        def fills_before(i, n, slots=SLOTS):
            return i * (4 + (0 if n else slots)) + (2 + (0 if n else slots))

        block = ctx.enter_context(nc.Block())

        @block.sync
        def _(sp):
            def slab(q, src, width=SLAB):
                if q >= 3:
                    filled(sp, last_use[q - 3])
                sp.dma_start(raw[:, slab_slot(q), :, 0:width], src).then_inc(raw_in[slab_slot(q)], 16)

            sp.dma_start(xT[:, :, 0:512], a["xT"][:, :, 0:512]).then_inc(x_in[0], 16)
            slab(0, a["w_qi"])
            sp.dma_start(xT[:, :, 512:S], a["xT"][:, :, 512:S]).then_inc(x_in[1], 16)
            slab(1, a["w_ks"], P + SMALL)
            slab(2, a["w_qa"])
            slab(3, a["w_u"])
            slab(4, a["w_v"])
            slab(5, a["w_z"])
            filled(sp, ("z", NT - 1))
            sp.dma_start(w_ukv[:, :, :], a["w_ukv"]).then_inc(wm_in, 16)
            sp.dma_start(w_m[:, :, :, :], a["w_m"]).then_inc(wm_in, 16)
            slab(6, a["w_out"][0])
            slab(7, a["w_out"][1])
            def half_slabs(j, src):
                for part, s in enumerate((raw_in, rest_in)):
                    ks = slice(4 * part, 4 * part + 4)
                    sp.dma_start(raw[:, (j + 2) % 3, ks, :], src[:, ks, :]).then_inc(s[(j + 2) % 3], 16)

            filled(sp, last_use[5])
            half_slabs(0, a["w_gu"][0])
            filled(sp, ("L", NT * AH - 1, 1))
            copied(sp, ("L", NT * AH - 1, 1))
            for g in range(4):
                sp.dma_start(h1all[:, 2 * g:2 * g + 2, :], a["x"][:, 2 * g:2 * g + 2, :]).then_inc(xres_in, 16)
            for q in range(9, 11):
                filled(sp, last_use[q - 3])
                half_slabs(q - NPRE, a["w_gu"][q - NPRE])
            for t in range(NT):
                sp.wait_ge(h1_done, t + 1)
                sp.dma_start(hext[t * P:(t + 1) * P, 0:D], h1all[:, t, :]).then_inc(h_out, 16)
            sp.wait_ge(gates_done, 1)
            sp.dma_start(hext[:, D:HROW].rearrange("(t p) e -> p t e", p=P), gates[:, :, :]).then_inc(gate_out, 16)
            for t in range(NT):
                sp.wait_ge(acc_half, t + 1)
                sp.dma_start(acc[t * P:(t + 1) * P, :], accst[:, t % 2, :]).then_inc(acc_out[t % 2], 16)
            sp.wait_ge(table_done, 1)
            entry = item_table(sp)
            n = sp.value_load(table[0:1, 3 * MAX_ITEMS:3 * MAX_ITEMS + 1], min_val=NE, max_val=MAX_ITEMS)

            def load_slab(i, e, j):
                src = a["w_gu"][bass.ds(e * 4 + j, 1)] if j < 4 else a["w_dn"][bass.ds(e * 2 + (j - 4), 1)]
                src = src.rearrange("o p k c -> p (o k) c")
                for part, s in enumerate((raw_in, rest_in)):
                    ks = slice(4 * part, 4 * part + 4)
                    last = (j + 3) % 6
                    lo, lo3 = i * 18 + (3 * last + 2 + part), i * 6 + (last + 1)
                    sp.wait_ge(lo_done, lo)
                    if part:
                        sp.sem_inc(sp_passed, 1)
                        sp.wait_ge(lo3_done, lo3)
                    sp.dma_start(raw[:, (j + 2) % 3, ks, :], src[:, ks, :]).then_inc(s[(j + 2) % 3], 16)

            with sp.Fori(0, n) as i:
                e, ex = entry(0, i, NE - 1), entry(0, i + 1, NE - 1)
                for j in (3, 4, 5):
                    load_slab(i, e, j)
                for j in (0, 1):
                    load_slab(i, ex, j)
                with sp.If(i + 1 < n):
                    load_slab(i, ex, 2)
            for g in (2, 3):
                piece_split(sp, n, 1, g)
            sp.wait_ge(all_added, 1)
            for g in range(2):
                sp.dma_start(fin[:, 4 * g:4 * g + 4, :],
                             acc[g * 512:(g + 1) * 512, :].rearrange("(t p) d -> p t d", p=P)).then_inc(fin_in[g], 16)
            for t in range(NT):
                sp.wait_ge(f_done, t + 1)
                sp.dma_start(out[0, t * P:(t + 1) * P, :], fin[:, t, :]).then_inc(f_out, 16)
            sp.wait_ge(f_out, 16 * NT)

        @block.tensor
        def _(pe):
            def opened(task):
                b, u = PLACE[task]
                if u:
                    pe.wait_ge(out_of[b], u)
                return ps[b]

            def closes(ins, task):
                ins.then_inc(full[PLACE[task][0]], 1)

            def slab_ready(q):
                pe.wait_ge(raw_in[slab_slot(q)], 16 * (q // 3 + 1))
                return raw[:, slab_slot(q), :, :]

            def feature_major(name, q, order=tuple((m, n) for n in range(2) for m in range(4))):
                w = slab_ready(q)
                for m, n in order:
                    if name == "qi" and m == 0:
                        pe.wait_ge(x_in[n], 16)
                    task = (name, m, n) if name != "ki" else (name, n)
                    b = opened(task)
                    for k in range(KT):
                        ins = pe.matmul(b[:, :], w[:, k, m * P:(m + 1) * P], xT[:, k, n * 512:(n + 1) * 512],
                                        start=k == 0, stop=k == KT - 1)
                    closes(ins, task)

            def token_major(name, q, col, width, per_bank):
                w = slab_ready(q)
                for j in range(NT // per_bank):
                    b = opened((name, j))
                    for i in range(per_bank):
                        t = j * per_bank + i
                        for k in range(KT):
                            ins = pe.matmul(b[:, i * width:(i + 1) * width], xT[:, k, t * P:(t + 1) * P],
                                            w[:, k, col:col + width], start=k == 0, stop=k == KT - 1)
                    closes(ins, (name, j))

            pe.wait_ge(consts_in, 32)
            feature_major("qi", 0)
            feature_major("ki", 1, [(0, 0), (0, 1)])
            token_major("small", 1, P, SMALL, 2)
            for n in range(2):
                for m in range(4):
                    copied(pe, ("qi", m, n))
                copied(pe, ("ki", n))
            for t in range(2, NT):
                for h in range(AH):
                    lo, m = AD * (h % 2), h // 2
                    for c, (k0, k1) in enumerate(chunks(t)):
                        b = opened(("sc", t, h, c))
                        closes(pe.matmul(b[:, 0:k1 - k0], qiT[lo:lo + AD, m, t * P:(t + 1) * P],
                                         kiT[lo:lo + AD, k0:k1], start=True, stop=True), ("sc", t, h, c))
            b = opened(("grow",))
            pe.wait_ge(lf_done, 1)
            pe.transpose(b[0:32, 0:P], gates_in[:, 0, :], ident)
            closes(pe.transpose(b[0:32, P:2 * P], gates_in[:, 2, :], ident), ("grow",))
            feature_major("qa", 2)
            b = opened(("grow2",))
            pe.wait_ge(rows_done, 1)
            pe.transpose(b[0:1, 0:32], g_b[:, P - 1:P], ident[0:32, 0:32])
            closes(pe.transpose(b[0:1, 32:64], g_tmp[:, P - 1:P], ident[0:32, 0:32]), ("grow2",))
            b = opened(("mprev",))
            pe.wait_ge(mrow_done, 1)
            closes(pe.matmul(b[0:32, 0:2], g_rowbuf[:, 3, :], onesf[0:1, 0:2], start=True, stop=True), ("mprev",))
            feature_major("u", 3)
            b = opened(("gcol",))
            pe.wait_ge(gexp_done, 1)
            pe.wait_ge(diag_done, 1)
            for k, rows in enumerate((g_r, g_e1, g_e2, g_w)):
                pe.transpose(b[:, 32 * k:32 * k + 32], rows[:, :], ident[0:32, 0:32])
            closes(pe.matmul(b[:, 128:160], onesf[0:32, :], g_diag[:, :], start=True, stop=True), ("gcol",))
            token_major("v", 4, 0, SLAB, 1)
            token_major("z", 5, 0, SLAB, 1)
            pe.wait_ge(rms_done, 1)
            for j in range(2):
                b = opened(("ct", j))
                for i in range(4):
                    ins = pe.transpose(b[:, i * P:(i + 1) * P], sm[:, 4 * j + i, 0:R], ident)
                closes(ins, ("ct", j))
            pe.wait_ge(wm_in, 32)
            pe.wait_ge(uc_ready, 4)
            copied(pe, ("gcol",))
            for c in range(NT):
                tok = slice(c * P, (c + 1) * P)
                for k, name in enumerate(("mq", "mk", "mkt")):
                    b = opened((name, c))
                    for h in range(MH):
                        w, u = w_m[:, min(k, 1), h, :], ucT[:, h, tok]
                        ins = pe.matmul(b[:, h * P:(h + 1) * P], w if k < 2 else u, u if k < 2 else w,
                                        start=True, stop=True)
                    closes(ins, (name, c))
                b = opened(("R", c))
                for h in range(MH):
                    row = ident[0:32, h * 8 + c:h * 8 + c + 1].to_broadcast([32, P])
                    ins = pe.matmul(b[:, h * P:(h + 1) * P], row, g_ng[:, :], start=True, stop=True)
                closes(ins, ("R", c))
                b = opened(("S", c))
                copied(pe, ("mq", c))
                copied(pe, ("mk", c))
                for h in range(MH):
                    ins = pe.matmul(b[:, h * P:(h + 1) * P], mqk[:, 1, h, :], mqk[:, 0, h, :], start=True, stop=True)
                closes(ins, ("S", c))
                for q in range(2 if c else 0):
                    b = opened(("X", c, q))
                    copied(pe, ("U", c - 1, q))
                    for h in (2 * q, 2 * q + 1):
                        ins = pe.matmul(b[:, (h % 2) * 129:(h % 2) * 129 + 129], mqk[:, 0, h, :], mC[:, h, :],
                                        start=True, stop=True)
                    closes(ins, ("X", c, q))
                copied(pe, ("v", c))
                pe.wait_ge(ones_set, 1)
                copied(pe, ("S", c))
                for q in range(2):
                    b = opened(("I", c, q))
                    for h in (2 * q, 2 * q + 1):
                        ins = pe.matmul(b[:, (h % 2) * 129:(h % 2) * 129 + 129], ma[:, h, :], vaug[:, c, h, :],
                                        start=True, stop=True)
                    closes(ins, ("I", c, q))
                for q in range(2 if c < NT - 1 else 0):
                    b = opened(("U", c, q))
                    copied(pe, ("mkt", c))
                    pe.wait_ge(wv_done, c + 1)
                    for h in (2 * q, 2 * q + 1):
                        ins = pe.matmul(b[:, (h % 2) * 129:(h % 2) * 129 + 129], mqk[:, 2, h, :], mwv[:, h, :],
                                        start=True, stop=True)
                    closes(ins, ("U", c, q))
            for c in range(NT):
                b = opened(("mt", c))
                pe.wait_ge(mout, c + 1)
                for h in range(MH):
                    ins = pe.transpose(b[:, h * P:(h + 1) * P], zs[:, c, h, :], ident)
                closes(ins, ("mt", c))
            for j in range(2):
                copied(pe, ("ct", j))
            for n in range(2):
                for m in range(4):
                    b = opened(("kt", m, n))
                    closes(pe.matmul(b[:, :], w_ukv[:, 0, m * P:(m + 1) * P], cT[:, n * 512:(n + 1) * 512],
                                     start=True, stop=True), ("kt", m, n))
            for t in range(NT):
                b = opened(("V", t))
                closes(pe.matmul(b[:, :], cT[:, t * P:(t + 1) * P], w_ukv[:, 1, :], start=True, stop=True), ("V", t))
            for n in range(2):
                for m in range(4):
                    copied(pe, ("kt", m, n))
            for n in range(NT * AH + 4):
                if n < NT * AH:
                    t, h = divmod(n, AH)
                    lo, m = AD * (h % 2), h // 2
                    for c, (k0, k1) in enumerate(chunks(t)):
                        b = opened(("L", n, c))
                        closes(pe.matmul(b[:, 0:k1 - k0], qaT[lo:lo + AD, m, t * P:(t + 1) * P],
                                         KTr[lo:lo + AD, m, k0:k1], start=True, stop=True), ("L", n, c))
                if 1 <= n <= NT * AH:
                    pe.wait_ge(p_ready, n)
                    for g, (j0, j1) in enumerate(groups((n - 1) // AH)):
                        b = opened(("T", n - 1, g))
                        for j in range(j0, j1):
                            ins = pe.transpose(b[:, (j - j0) * P:(j - j0 + 1) * P],
                                               Lp[:, (n - 1) % 3, j * P:(j + 1) * P], ident)
                        closes(ins, ("T", n - 1, g))
                if 2 <= n < NT * AH + 2:
                    t, h = divmod(n - 2, AH)
                    if h == 0:
                        copied(pe, ("V", t))
                        if t:
                            pe.wait_ge(o_copied, t)
                    for g in range(len(groups(t))):
                        copied(pe, ("T", n - 2, g))
                    for j in range(t + 1):
                        ins = pe.matmul(ps[NB][:, h * AD:(h + 1) * AD], pT[:, (n - 2) % 2, j, :],
                                        Vn[:, j, h * AD:(h + 1) * AD], start=j == 0, stop=j == t)
                    if h == AH - 1:
                        ins.then_inc(o_full, 1)
                if n >= 11 and n % AH == 3:
                    t = n // AH - 1
                    b = opened(("at", t))
                    pe.wait_ge(o_copied, t + 1)
                    for j in range(4):
                        ins = pe.transpose(b[:, j * P:(j + 1) * P], ao[:, j * P:(j + 1) * P], ident)
                    closes(ins, ("at", t))

            def mix(t):
                for n in range(2):
                    w = slab_ready(6 + n)
                    b = opened(("mix", t, n))
                    for k in range(KT):
                        ins = pe.matmul(b[:, :], catT[:, k, t * P:(t + 1) * P], w[:, k, :],
                                        start=k == 0, stop=k == KT - 1)
                    closes(ins, ("mix", t, n))

            def h_turned(t):
                pe.wait_ge(h1_done, t + 1)
                for g in range(2):
                    b = opened(("ht", t, g))
                    for k in range(4):
                        ins = pe.transpose(b[:, k * P:(k + 1) * P], h1all[:, t, (4 * g + k) * P:(4 * g + k + 1) * P],
                                           ident)
                    closes(ins, ("ht", t, g))

            def router(t):
                b = opened(("rt", t))
                for g in range(2):
                    copied(pe, ("ht", t, g))
                for k in range(KT):
                    ins = pe.matmul(b[0:NE, 0:P], w_rt[:, k, :], h1T[:, t % 2, k, :], start=k == 0, stop=k == KT - 1)
                closes(ins, ("rt", t))
                b = opened(("rtt", t))
                copied(pe, ("rt", t))
                closes(pe.transpose(b[:, 0:NE], lgT[:, t % 2, :], ident[0:NE, 0:NE]), ("rtt", t))

            for t in range(NT):
                copied(pe, ("at", t))
                copied(pe, ("mt", t))
            pe.wait_ge(lnp_in, 80)
            for t in range(NT):
                mix(t)
                if t:
                    h_turned(t - 1)
                if t > 1:
                    router(t - 2)
            h_turned(NT - 1)
            router(NT - 2)
            router(NT - 1)
            b = opened(("cnt",))
            pe.wait_ge(picks_done, 1)
            pe.matmul(b[:, 0:256], cb[:, 0:P], picks_b[:, :, :].rearrange("p t e -> p (t e)"), start=True, stop=True)
            closes(pe.matmul(b[:, 256:512], cb[:, P:2 * P], picks_b[:, :, :].rearrange("p t e -> p (t e)"),
                             start=True, stop=True), ("cnt",))
            b = opened(("items",))
            pe.wait_ge(items_done, 1)
            pe.transpose(b[0:1, 0:P], rt_c[:, 0:1], ident)
            closes(pe.transpose(b[0:1, P:2 * P], rt_c[:, 1:2], ident), ("items",))
            for j in range(2):
                b = opened(("gt", j))
                for i in range(4):
                    ins = pe.transpose(b[0:NE, i * P:(i + 1) * P], gates[:, 4 * j + i, :], ident)
                closes(ins, ("gt", j))
            for t in range(NT):
                copied(pe, ("gt", t // 4))
                for n in range(2):
                    b = opened(("bd", t, n))
                    closes(pe.matmul(b[:, :], GT[:, t * P:(t + 1) * P], bdown[:, n * 512:(n + 1) * 512],
                                     start=True, stop=True), ("bd", t, n))

            for b in range(NB):
                pe.wait_ge(out_of[b], len([1 for v in PLACE.values() if v[0] == b]))
            pe.wait_ge(table_done, 1)
            entry = item_table(pe)
            n_items = pe.value_load(table[0:1, 3 * MAX_ITEMS:3 * MAX_ITEMS + 1], min_val=NE, max_val=MAX_ITEMS)

            def product(bank_ap, hi_buf, lo_buf, b, k, slot, col, start, stop):
                hi, lo = hi_buf[:, k, b * P:(b + 1) * P], lo_buf[:, k, b * P:(b + 1) * P]
                pe.matmul(bank_ap, hi, whi[:, slot, col, :], start=start, stop=False)
                pe.matmul(bank_ap, hi, wlo[:, slot, col, :], start=False, stop=False)
                return pe.matmul(bank_ap, lo, whi[:, slot, col, :], start=False, stop=stop)

            def find_slots(item, fill):
                pe.wait_ge(slots_done, item + 1)
                if fill > 1:
                    pe.wait_ge(tr_free[0], fill - 1)
                for b in range(2):
                    for t in range(NT):
                        ins = pe.matmul(ps[TR_BANK[0]][:, 4 * b:4 * b + 3], slots[:, t, b * P:(b + 1) * P],
                                        cb[:, 2 * P + 3 * t:2 * P + 3 * t + 3], start=t == 0, stop=t == NT - 1)
                ins.then_inc(tr_full[0], 1)

            def turn(src, blocks, pair, fill, first=False):
                if not first:
                    pe.wait_ge(tr_free[pair % 2], fill - 1)
                for k in range(2):
                    for b in blocks:
                        ins = pe.transpose(ps[TR_BANK[pair % 2]][:, (2 * k + b) * P:(2 * k + b + 1) * P],
                                           src[:, b, (2 * pair + k) * P:(2 * pair + k + 1) * P], ident)
                ins.then_inc(tr_full[pair % 2], 1)

            def gate_up(j, i, n1, blocks):
                for b in blocks:
                    if j == 0 and b == blocks[0]:
                        pe.wait_ge(tr_free[0], fills_before(i, 0))
                        pe.wait_ge(tr_free[1], fills_before(i, 1))
                    bank_n, uses = gu_place(b, j, i, n1, blocks)
                    pe.wait_ge(gu_read[bank_n], since(uses))
                    for k in range(KT):
                        if k % 2 == 0 and b == blocks[0]:
                            piece_split(pe, i, j, k // 2)
                        ins = product(ps[bank_n][:, :], xhi, xlo, b, k, j % 2, k, k == 0, k == KT - 1)
                        if b == 0 and k % 2:
                            ins.then_inc(piece_used, 1)
                    if b:
                        ins.then_inc(gu_full1, 1)

            def down(ks, i, n1, blocks):
                j = 4 + ks[0] // 4
                for b in blocks:
                    if ks[0] == 0:
                        pe.wait_ge(y_done[b], since(n1 * 2 if b else i * 2))
                    for k in ks:
                        if b == blocks[0]:
                            piece_split(pe, i, j, k % 4)
                        for n in range(2):
                            ins = product(ps[Y_BANK[b][n]][:, :], hhi, hlo, b, k, j % 2, 2 * (k % 4) + n,
                                          k == 0, k == KT - 1)
                        if b == 0:
                            ins.then_inc(piece_used, 1)
                    if b and ks[-1] == KT - 1:
                        ins.then_inc(y_full1, 1)

            def turn_h(quarter, i, n1, blocks):
                for b in blocks:
                    pe.wait_ge(hb_done[b], since((n1 if b else i) * 4 + (quarter + 1)))
                turn(hb, blocks, quarter, fill_of(i, "h", quarter))

            def item(i, n1, blocks):
                gate_up(0, i, n1, blocks)
                find_slots(i + 1, fills_before(i, 0) + 1)
                gate_up(1, i, n1, blocks)
                gate_up(2, i, n1, blocks)
                turn_h(0, i, n1, blocks)
                turn_h(1, i, n1, blocks)
                gate_up(3, i, n1, blocks)
                turn_h(2, i, n1, blocks)
                for quarter in range(2):
                    pe.wait_ge(tr_free[quarter], fill_of(i, "h", quarter))
                down(range(0, 2), i, n1, blocks)
                pe.wait_ge(tokens_in, i + 2)
                for pair in range(2):
                    turn(xg, (1, 0), pair, fill_of(i, "x", pair))
                down(range(2, 4), i, n1, blocks)
                turn_h(3, i, n1, blocks)
                pe.wait_ge(tr_free[0], fill_of(i, "h", 2))
                down(range(4, 6), i, n1, blocks)
                turn(xg, (1, 0), 2, fill_of(i, "x", 2))
                turn(xg, (1, 0), 3, fill_of(i, "x", 3))
                down(range(6, 8), i, n1, blocks)

            find_slots(0, 1)
            pe.wait_ge(tokens_in, 1)
            for pair in range(4):
                turn(xg, (1, 0), pair, (2, 1, 3, 2)[pair], first=pair == 1)
            with pe.Fori(0, n_items) as i:
                b1, n1 = entry(1, i, 1), entry(2, i, MAX_ITEMS)
                with pe.If(b1 > 0):
                    item(i, n1, (1, 0))
                with pe.If(b1 < 1):
                    item(i, n1, (0,))

        @block.scalar
        def _(act):
            def copy_out(task, dst, src, func=ACT.Copy, **kw):
                frees(act.activation(dst, src, func, **kw), task)

            act.dma_start(consts[:, :], a["consts"]).then_inc(consts_in, 16)
            act.dma_start(cb[:, :], a["cb"]).then_inc(consts_in, 16)
            act.dma_start(small_b[:, :], a["b_if"].partition_broadcast(P)).then_inc(bias_in, 16)
            act.dma_start(g_kv[:, :], a["kv_norm_g"]).then_inc(late_in, 16)
            act.dma_start(convw[:, :, :], a["conv"]).then_inc(late_in, 16)
            act.wait_ge(consts_in, 32)
            for n in range(2):
                for m in range(4):
                    b = filled(act, ("qi", m, n))
                    copy_out(("qi", m, n), qiT[:, m, n * 512:(n + 1) * 512], b[:, :])
            for n in range(2):
                copy_out(("ki", n), kiT[:, n * 512:(n + 1) * 512], filled(act, ("ki", n))[:, :])
            act.wait_ge(lf_in, 3)
            act.activation(gates_in[:, 2, :], gates_in[:, 2, :], ACT.Exp).then_inc(lf_exp, 1)
            act.wait_ge(lf_exp, 1)
            act.activation(gates_in[:, 2, :], gates_in[:, 2, :], ACT.Ln, bias=1.0).then_inc(lf_ln, 1)
            act.wait_ge(rms_sum, NT)
            act.activation(rms_tmp[:, 1, :], rms_tmp[:, 0, :], ACT.Sqrt, scale=1.0 / R, bias=consts[:, C_COL + 1:C_COL + 2]).then_inc(rms_root, 1)
            r = 0
            for t in range(2, NT):
                for h in range(AH):
                    if r >= 2:
                        act.wait_ge(score_acc, r - 1)
                    for c, (k0, k1) in enumerate(chunks(t)):
                        b = filled(act, ("sc", t, h, c))
                        copy_out(("sc", t, h, c), rel[:, r % 2, k0:k1], b[:, 0:k1 - k0], ACT.Relu)
                    r += 1
            act.dma_start(normg[:, :], a["m_norm_g"].partition_broadcast(P)).then_inc(normg_in, 16)
            for n in range(2):
                for m in range(4):
                    b = filled(act, ("qa", m, n))
                    copy_out(("qa", m, n), qaT[:, m, n * 512:(n + 1) * 512], b[:, :], scale=consts[:, C_QS + m:C_QS + m + 1])
            for n in range(2):
                for m in range(4):
                    b = filled(act, ("u", m, n))
                    copy_out(("u", m, n), uT[:, m, 3 + n * 512:3 + (n + 1) * 512], b[:, :])
            act.wait_ge(g_done, 1)
            act.activation(g_e1[:, :], g_g[:, :], ACT.Exp, scale=-1.0, bias=g_col[:, 0:1]).then_inc(gexp_step, 1)
            act.activation(g_e2[:, :], g_tmp[:, :], ACT.Exp, scale=-1.0).then_inc(gexp_step, 1)
            act.activation(g_w[:, :], g_r[:, :], ACT.Exp, bias=g_ng[:, P - 1:P]).then_inc(gexp_step, 1)
            act.activation(g_col[:, 1:2], g_col[:, 0:1], ACT.Exp, bias=g_ng[:, P - 1:P]).then_inc(gexp_done, 1)
            for t in range(NT):
                b = filled(act, ("v", t))
                copy_out(("v", t), vaug[:, t, :, 0:MD], b[:, :].rearrange("p (h d) -> p h d", h=4))
            for m in range(4):
                act.wait_ge(conv_done, m + 1)
                act.activation(ucT[:, m, :], ucT[:, m, :], ACT.Silu, bias=convw[:, m, 4:5]).then_inc(uc_ready, 1)
            for t in range(NT):
                b = filled(act, ("z", t))
                copy_out(("z", t), zs[:, t, :, :], b[:, :].rearrange("p (h d) -> p h d", h=4), ACT.Sigmoid)
            for j in range(2):
                b = filled(act, ("ct", j))
                copy_out(("ct", j), cT[:, j * 512:(j + 1) * 512], b[:, :], scale=g_kv[:, 0:1])
            for c in range(NT):
                for k, name in enumerate(("mq", "mk", "mkt")):
                    b = filled(act, (name, c))
                    copy_out((name, c), mqk[:, k, :, :], b[:, :].rearrange("p (h d) -> p h d", h=4),
                             scale=1.0 if k == 0 else MD ** -0.5)
                copied(act, ("R", c))
                for h in range(MH):
                    act.activation(ma[:, h, :], ma[:, h, :], ACT.Exp, bias=gate_cols[:, 0, h * 8 + c:h * 8 + c + 1])\
                       .then_inc(gate_exp, 1)
                for q in range(2 if c else 0):
                    b = filled(act, ("X", c, q))
                    copied(act, ("I", c - 1, q))
                    h = 2 * q
                    act.activation(mst[:, h, :], b[:, 0:129], ACT.Copy, scale=gate_cols[:, 1, h * 8 + c:h * 8 + c + 1])\
                       .then_inc(x_part, 1)
                    h = 2 * q + 1
                    copy_out(("X", c, q), mst[:, h, :], b[:, 129:258], scale=gate_cols[:, 1, h * 8 + c:h * 8 + c + 1])
            act.wait_ge(mvar_done, 1)
            act.activation(m_rstd[:, :, :], m_rstd[:, :, :], ACT.Sqrt).then_inc(mroot, 1)
            act.wait_ge(mnorm_in, 2)
            for c in range(NT):
                for h in range(MH):
                    act.activation(vaug[:, c, h, 0:MD], vaug[:, c, h, 0:MD], ACT.Identity,
                                   scale=m_rstd[:, c, h:h + 1], bias=m_nmr[:, c, h:h + 1]).then_inc(mnormed, 1)
            for c in range(NT):
                b = filled(act, ("mt", c))
                copy_out(("mt", c), catT[:, 4:8, c * P:(c + 1) * P], b[:, :].rearrange("p (h d) -> p h d", h=4))
            for n in range(2):
                for m in range(4):
                    copy_out(("kt", m, n), KTr[:, m, n * 512:(n + 1) * 512], filled(act, ("kt", m, n))[:, :])
            for t in range(NT):
                copy_out(("V", t), Vn[:, t, :], filled(act, ("V", t))[:, :])
            for n in range(NT * AH + 4):
                if n < NT * AH:
                    t, h = divmod(n, AH)
                    act.wait_ge(att_shift, n + 1)
                    act.activation(Lp[:, n % 3, 0:P * (t + 1)], Lp[:, n % 3, 0:P * (t + 1)], ACT.Exp,
                                   scale=2.0 ** -(h + 1), bias=att_bias[:, n % 3:n % 3 + 1],
                                   accum_out=att_sum[:, t % 2, h:h + 1]).then_inc(p_ready, 1)
                if 1 <= n <= NT * AH:
                    j0, j1 = groups((n - 1) // AH)[0]
                    b = filled(act, ("T", n - 1, 0))
                    copy_out(("T", n - 1, 0), pT[:, (n - 1) % 2, j0:j1, :],
                             b[:, 0:(j1 - j0) * P].rearrange("p (j q) -> p j q", q=P))
                if n >= 11 and n % AH == 3:
                    t = n // AH - 1
                    b = filled(act, ("at", t))
                    copy_out(("at", t), catT[:, 0:4, t * P:(t + 1) * P], b[:, :].rearrange("p (j q) -> p j q", q=P))
            act.dma_start(lnp[:, 0, :], a["ln1_g"].partition_broadcast(P)).then_inc(lnp_in, 16)
            act.dma_start(lnp[:, 1, :], a["ln1_b"].partition_broadcast(P)).then_inc(lnp_in, 16)
            act.dma_start(bdown[:, :], a["b_down"]).then_inc(lnp_in, 16)
            act.dma_start(w_rt[:, :, :], a["w_router"]).then_inc(lnp_in, 16)
            act.dma_start(br[:, :], a["b_router"].partition_broadcast(P)).then_inc(lnp_in, 16)

            def ln1_root(t):
                act.wait_ge(ln_var, t + 1)
                act.activation(ln_rstd[:, t % 2, 0:1], ln_mv[:, t % 2, 1:2], ACT.Sqrt, bias=consts[:, C_COL + 1:C_COL + 2])\
                   .then_inc(ln_root, 1)
                act.wait_ge(ln_sb, t + 1)
                act.activation(h1all[:, t, :], h1all[:, t, :], ACT.Identity, scale=ln_rstd[:, t % 2, 0:1],
                               bias=ln_rstd[:, t % 2, 1:2]).then_inc(ln_norm, 1)

            def turned(t):
                for g in range(2):
                    b = filled(act, ("ht", t, g))
                    copy_out(("ht", t, g), h1T[:, t % 2, 4 * g:4 * g + 4, :], b[:, :].rearrange("p (j q) -> p j q", q=P))

            def router_out(t):
                b = filled(act, ("rt", t))
                copy_out(("rt", t), lgT[:, t % 2, :], b[0:NE, 0:P])

            for t in range(NT):
                ln1_root(t)
                if t:
                    turned(t - 1)
                if t > 1:
                    router_out(t - 2)
            turned(NT - 1)
            router_out(NT - 2)
            router_out(NT - 1)
            act.wait_ge(rt_diff, 1)
            act.activation(gexp[:, :, :], gexp[:, :, :], ACT.Exp).then_inc(rt_exp, 1)
            for j in range(2):
                b = filled(act, ("gt", j))
                copy_out(("gt", j), GT[:, j * 512:(j + 1) * 512], b[0:NE, :])

            act.wait_ge(table_done, 1)
            entry = item_table(act)
            n_items = act.value_load(table[0:1, 3 * MAX_ITEMS:3 * MAX_ITEMS + 1], min_val=NE, max_val=MAX_ITEMS)

            def biases(e, seen):
                act.wait_ge(gu_read[0], since(seen))
                act.wait_ge(gu_read[1], since(seen))
                act.dma_start(bgu[:, :], a["b_gu"][bass.ds(e, 1), :].rearrange("o c -> (o c)").partition_broadcast(P))\
                   .then_inc(bgu_in, 16)

            def take_hi(j, pieces, i=0):
                for g in pieces:
                    act.wait_ge((raw_in if g < 2 else rest_in)[(j + 2) % 3],
                                (i * 2 + ((NPRE + j) // 3 + 1 if g < 2 else j // 3 + 1)) * 16)
                    if j >= 2:
                        act.wait_ge(piece_used, i * 24 + (4 * (j - 2) + g + 1))
                    act.activation(whi[:, j % 2, 2 * g:2 * g + 2, :], raw[:, (j + 2) % 3, 2 * g:2 * g + 2, :], ACT.Copy)\
                       .then_inc(hi_done, 1)

            def turned_hi(dst, pair, fill, width=2):
                n, w = pair % 2, width * P
                act.wait_ge(tr_full[n], fill)
                act.activation(dst[:, 2 * pair:2 * pair + 2, 0:w],
                               ps[TR_BANK[n]][:, :].rearrange("p (k q) -> p k q", q=2 * P)[:, :, 0:w],
                               ACT.Copy).then_inc(tr_hi[n], 1)

            def sigmoid(quarter, i, n1, blocks):
                for b in blocks:
                    act.wait_ge(clip_g[b], (n1 if b else i) * 4 + (quarter + 1))
                    act.activation(hb[:, b, quarter * 256:(quarter + 1) * 256], gu[:, b, quarter % 2, 0:256],
                                   ACT.Sigmoid, scale=1.702).then_inc(sig_done[b], 1)

            def item(i, n1, n1x, ex, blocks):
                act.activation(act_tmp[:, :], act_tmp[:, :], ACT.Sigmoid).then_inc(act_table, 1)
                take_hi(2, (0,), i)
                for j in range(4):
                    if j < 3:
                        sigmoid(j, i, n1, blocks[:-1])
                    take_hi(j + 2, (1, 2, 3), i)
                    if j == 2:
                        turned_hi(hhi, 0, fill_of(i, "h", 0), len(blocks))
                        turned_hi(hhi, 1, fill_of(i, "h", 1), len(blocks))
                    if j == 3:
                        turned_hi(hhi, 2, fill_of(i, "h", 2), len(blocks))
                    if len(blocks) == 2:
                        sigmoid(j, i, n1, blocks[-1:])
                    if j == 2 and len(blocks) == 2:
                        sigmoid(3, i, n1, blocks[:-1])
                    take_hi(j + 3, (0,), i)
                    if len(blocks) == 1:
                        sigmoid(j, i, n1, blocks[-1:])
                take_hi(6, (1,), i)
                for pair in range(2):
                    turned_hi(xhi, pair, fill_of(i, "x", pair))
                take_hi(6, (2,), i)
                biases(ex, i * 2 + n1x * 2 + 2)
                take_hi(6, (3,), i)
                turned_hi(hhi, 3, fill_of(i, "h", 3), len(blocks))
                take_hi(7, (0, 1), i)
                turned_hi(xhi, 2, fill_of(i, "x", 2))
                turned_hi(xhi, 3, fill_of(i, "x", 3))
                take_hi(7, (2, 3), i)
                for b in blocks:
                    for n in range(2):
                        if n == 0:
                            act.wait_ge(gate_cp, i + 1)
                            act.wait_ge(sum_kept, i + 1)
                        if b:
                            act.wait_ge(y_full1, n1 + 1)
                        act.activation(ysb[:, b, n * SLAB:(n + 1) * SLAB], ps[Y_BANK[b][n]][:, :], ACT.Copy,
                                       scale=gcol[:, b:b + 1]).then_inc(y_done[b], 1)

            starts(act, y_done)
            act.activation(act_tmp[:, :], consts[:, C_COL:C_COL + 1], ACT.Copy).then_inc(act_table, 1)
            act.wait_ge(act_table, 1)
            act.dma_start(bgu[:, :], a["b_gu"][0:1, :].rearrange("o c -> (o c)").partition_broadcast(P)).then_inc(bgu_in, 16)
            for b in range(NB):
                act.wait_ge(out_of[b], len([1 for v in PLACE.values() if v[0] == b]))
            take_hi(0, range(4))
            take_hi(1, range(4))
            for pair in range(4):
                turned_hi(xhi, pair, (2, 1, 3, 2)[pair])
            with act.Fori(0, n_items) as i:
                b1, n1 = entry(1, i, 1), entry(2, i, MAX_ITEMS)
                b1x, n1x = entry(1, i + 1, 1), entry(2, i + 1, MAX_ITEMS)
                ex = entry(0, i + 1, NE - 1)
                with act.If(b1 > 0):
                    item(i, n1, n1x, ex, (1, 0))
                with act.If(b1 < 1):
                    item(i, n1, n1x, ex, (0,))
            for g in (2, 3):
                piece_split(act, n_items, 1, g)
            act.wait_ge(all_added, 1)
            act.dma_start(lnq[:, 0, :], a["ln2_g"].partition_broadcast(P)).then_inc(lnq_in, 16)
            act.dma_start(lnq[:, 1, :], a["ln2_b"].partition_broadcast(P)).then_inc(lnq_in, 16)
            for t in range(NT):
                act.wait_ge(f_var, t + 1)
                act.activation(frs[:, 0, t:t + 1], fmv[:, t, 1:2], ACT.Sqrt, bias=consts[:, C_COL + 1:C_COL + 2])\
                   .then_inc(f_root, 1)
                act.wait_ge(f_sb, t + 1)
                act.activation(fin[:, t, :], fin[:, t, :], ACT.Identity, scale=frs[:, 0, t:t + 1],
                               bias=frs[:, 1, t:t + 1]).then_inc(f_norm, 1)

        @block.vector
        def _(dve):
            def heads(ap, width):
                return ap.unsqueeze(2).to_broadcast([P, 4, width])

            dve.wait_ge(consts_in, 32)
            dve.wait_ge(bias_in, 16)
            for j in range(4):
                b = filled(dve, ("small", j))
                frees(dve.tensor_copy(sm[:, 2 * j:2 * j + 2, :], b[:, 0:2 * SMALL].rearrange("p (t c) -> p t c", t=2)),
                      ("small", j))
            for j in range(4):
                copied(dve, ("small", j))
            for k in range(2):
                dve.tensor_tensor(gates_in[:, k, :].rearrange("p (h c) -> p h c", h=4),
                                  sm[:, :, R + 8 + 4 * k:R + 12 + 4 * k].rearrange("p c h -> p h c"),
                                  small_b[:, 4 * k:4 * k + 4].unsqueeze(2).to_broadcast([P, 4, NT]), ALU.add).then_inc(lf_in, 1)
            dve.wait_ge(lf_in, 2)
            dve.scalar_tensor_tensor(out=gates_in[:, 2, :], in0=gates_in[:, 1, :], scalar=-1.0, in1=gates_in[:, 1, :],
                                     op0=ALU.mult, op1=ALU.min).then_inc(lf_in, 1)
            for t in range(NT):
                dve.tensor_tensor_reduce(cT[:, t * P:(t + 1) * P], sm[:, t, 0:R], sm[:, t, 0:R], 1.0, 0.0,
                                         ALU.mult, ALU.add, rms_tmp[:, 0, t:t + 1]).then_inc(rms_sum, 1)
            dve.wait_ge(lf_ln, 1)
            dve.scalar_tensor_tensor(out=gates_in[:, 2, :], in0=gates_in[:, 1, :], scalar=0.0, in1=gates_in[:, 2, :],
                                     op0=ALU.min, op1=ALU.subtract).then_inc(lf_done, 1)
            dve.wait_ge(rms_root, 1)
            rstep = serial(dve, rms_step)
            rstep(dve.reciprocal(rms_tmp[:, 2, :], rms_tmp[:, 1, :]))
            dve.tensor_tensor(sm[:, :, 0:R], sm[:, :, 0:R], rms_tmp[:, 2, :].unsqueeze(2).to_broadcast([P, NT, R]),
                              ALU.mult).then_inc(rms_done, 1)
            r = 0
            for t in range(2, NT):
                sc = score_of(t)
                for h in range(AH):
                    for c in range(len(chunks(t))):
                        copied(dve, ("sc", t, h, c))
                    w = sm[:, t, R + h:R + h + 1]
                    if h:
                        dve.wait_ge(score_acc, r)
                        dve.scalar_tensor_tensor(out=sc, in0=rel[:, r % 2, 0:P * (t + 1)], scalar=w, in1=sc,
                                                 op0=ALU.mult, op1=ALU.add).then_inc(score_acc, 1)
                    else:
                        dve.tensor_scalar(sc, rel[:, r % 2, 0:P * (t + 1)], w, None, ALU.mult).then_inc(score_acc, 1)
                    r += 1
            gstep = serial(dve, gate_step)
            b = filled(dve, ("grow",))
            gstep(dve.tensor_copy(g_li[:, :], b[0:32, 0:P]))
            frees(dve.tensor_copy(g_e1[:, :], b[0:32, P:2 * P]), ("grow",))
            copied(dve, ("grow",))
            gstep(dve.tensor_tensor_scan(g_b[:, :], onesf[0:32, :], g_e1[:, :], 0.0, ALU.mult, ALU.add))
            gstep(dve.tensor_tensor(g_r[:, :], g_li[:, :], g_b[:, :], ALU.subtract))
            dve.tensor_tensor_scan(g_tmp[:, :], g_r[:, :], g_r[:, :], -3.0e38, ALU.max, ALU.max).then_inc(rows_done, 1)
            b = filled(dve, ("grow2",))
            frees(dve.tensor_copy(g_rowbuf[:, 0:2, :].rearrange("p a b -> p (a b)"), b[0:1, 0:64]), ("grow2",))
            copied(dve, ("grow2",))
            for h in range(MH):
                s = slice(h * 8, h * 8 + 8)
                gstep(dve.tensor_tensor_scan(g_rowbuf[:, 2, s], g_rowbuf[:, 1, s], g_rowbuf[:, 0, s], -1e30,
                                             ALU.max, ALU.add))
            gstep(dve.memset(g_rowbuf[:, 3, :], -1e30))
            dve.tensor_copy(g_rowbuf[:, 3, :].rearrange("p (h c) -> p h c", h=4)[:, :, 1:8],
                            g_rowbuf[:, 2, :].rearrange("p (h c) -> p h c", h=4)[:, :, 0:7]).then_inc(mrow_done, 1)
            b = filled(dve, ("mprev",))
            frees(dve.tensor_copy(g_col[:, 0:1], b[0:32, 0:1]), ("mprev",))
            copied(dve, ("mprev",))
            gstep(dve.tensor_scalar(g_g[:, :], g_tmp[:, :], g_col[:, 0:1], None, ALU.max))
            gstep(dve.tensor_scalar(g_ng[:, :], g_g[:, :], -1.0, None, ALU.mult))
            dve.tensor_tensor(g_tmp[:, :], g_b[:, :], g_g[:, :], ALU.add).then_inc(g_done, 1)
            dve.wait_ge(gexp_done, 1)
            dve.tensor_scalar(g_diag[:, :], ident[0:32, 0:32], g_col[:, 1:2], None, ALU.mult).then_inc(diag_done, 1)
            b = filled(dve, ("gcol",))
            frees(dve.tensor_copy(gate_cols[:, :, :].rearrange("p a b -> p (a b)"), b[:, 0:160]), ("gcol",))
            copied(dve, ("gcol",))

            tstep = serial(dve, topk_step)

            def selection():
                for t in range(NT):
                    sc, n = score_of(t), P * (t + 1)
                    if t < 2:
                        tstep(dve.tensor_copy(sc, dist_of(t)))
                        tstep(dve.memset(sc[0:64, n - 64:n], FAR))
                        continue
                    tstep(dve.memset(sc[0:64, n - 64:n], OUTSIDE))
                    for _ in range(TOPK // 8):
                        tstep(dve.max(top8[:, :], sc))
                        tstep(dve.match_replace(sc, top8[:, :], sc, PICKED))
                        yield
                    tstep(dve.tensor_scalar(sc, sc, PICKED, FAR, ALU.not_equal, ALU.mult))
                    tstep(dve.tensor_tensor(sc, sc, dist_of(t), ALU.max))
                    yield

            rounds = selection()

            def select(n):
                for _ in range(n):
                    next(rounds, None)

            hstep = serial(dve, ml_step)
            for c in range(NT):
                select(6)
                b = filled(dve, ("R", c))
                frees(dve.tensor_tensor(ma[:, :, :], b[:, :].rearrange("p (h t) -> p h t", h=4),
                                        cmask.unsqueeze(1).to_broadcast([P, 4, P]), ALU.add), ("R", c))
                select(6)
                b = filled(dve, ("S", c))
                dve.wait_ge(gate_exp, 4 * (c + 1))
                frees(dve.tensor_tensor(ma[:, :, :], b[:, :].rearrange("p (h t) -> p h t", h=4), ma[:, :, :], ALU.mult),
                      ("S", c))
                select(6)
                for q in range(2):
                    b = filled(dve, ("I", c, q))
                    part = b[:, 0:258].rearrange("p (h d) -> p h d", h=2)
                    if c:
                        copied(dve, ("X", c, q))
                        frees(dve.tensor_tensor(mnum[:, 2 * q:2 * q + 2, :], part, mst[:, 2 * q:2 * q + 2, :], ALU.add),
                              ("I", c, q))
                    else:
                        frees(dve.tensor_copy(mnum[:, 2 * q:2 * q + 2, :], part), ("I", c, q))
                for q in range(2 if c < NT - 1 else 0):
                    b = filled(dve, ("U", c, q))
                    part = b[:, 0:258].rearrange("p (h d) -> p h d", h=2)
                    if c:
                        dve.wait_ge(c_decayed, c)
                        frees(dve.tensor_tensor(mC[:, 2 * q:2 * q + 2, :], mC[:, 2 * q:2 * q + 2, :], part, ALU.add),
                              ("U", c, q))
                    else:
                        frees(dve.tensor_copy(mC[:, 2 * q:2 * q + 2, :], part), ("U", c, q))
                for q in range(2):
                    copied(dve, ("I", c, q))
                hstep(dve.scalar_tensor_tensor(out=m_den[:, 0, :], in0=mnum[:, :, MD], scalar=-1.0, in1=mnum[:, :, MD],
                                               op0=ALU.mult, op1=ALU.max))
                hstep(dve.tensor_tensor(m_den[:, 0, :], m_den[:, 0, :], gate_at(2, c), ALU.max))
                hstep(dve.reciprocal(m_den[:, 1, :], m_den[:, 0, :]))
                if c < NT - 1:
                    dve.wait_ge(wv_done, c + 1)
                hstep(dve.tensor_tensor(vaug[:, c, :, 0:MD], mnum[:, :, 0:MD], heads(m_den[:, 1, :], MD), ALU.mult))
                for h in range(MH):
                    dve.bn_stats(m_stat[:, h, :], vaug[:, c, h, 0:MD]).then_inc(h_written, 1)
                dve.wait_ge(h_written, 8 * c + 4)
                for h in range(MH):
                    dve.bn_aggr(m_mv[:, c, h, :], m_stat[:, h, :]).then_inc(h_written, 1)
                dve.wait_ge(h_written, 8 * c + 8)
            dve.tensor_scalar(m_rstd[:, :, :], m_mv[:, :, :, 1], EPS, None, ALU.add).then_inc(mvar_done, 1)
            select(6)
            dve.wait_ge(mroot, 1)
            dve.reciprocal(m_rstd[:, :, :], m_rstd[:, :, :]).then_inc(mnorm_in, 1)
            dve.wait_ge(mnorm_in, 1)
            dve.scalar_tensor_tensor(out=m_nmr[:, :, :], in0=m_mv[:, :, :, 0], scalar=-1.0, in1=m_rstd[:, :, :],
                                     op0=ALU.mult, op1=ALU.mult).then_inc(mnorm_in, 1)
            for _ in rounds:
                pass
            astep = serial(dve, att_step)
            for n in range(NT * AH + 4):
                if n < NT * AH:
                    t, h = divmod(n, AH)
                    ks = chunks(t)
                    for c, (k0, k1) in enumerate(ks):
                        b = filled(dve, ("L", n, c))
                        frees(dve.tensor_tensor_reduce(Lp[:, n % 3, k0:k1], b[:, 0:k1 - k0], score_of(t)[:, k0:k1], 1.0,
                                                       -3.0e38, ALU.subtract, ALU.max, att_m[:, n % 3, c:c + 1]),
                              ("L", n, c))
                    for c in range(len(ks)):
                        copied(dve, ("L", n, c))
                    dve.tensor_scalar(att_bias[:, n % 3:n % 3 + 1], att_m[:, n % 3, 0:1],
                                      att_m[:, n % 3, len(ks) - 1:len(ks)], -(2.0 ** -(h + 1)), ALU.max, ALU.mult)\
                       .then_inc(att_shift, 1)
                if 1 <= n <= NT * AH:
                    for g, (j0, j1) in list(enumerate(groups((n - 1) // AH)))[1:]:
                        b = filled(dve, ("T", n - 1, g))
                        frees(dve.tensor_copy(pT[:, (n - 1) % 2, j0:j1, :],
                                              b[:, 0:(j1 - j0) * P].rearrange("p (j q) -> p j q", q=P)), ("T", n - 1, g))
                if n >= 9 and n % AH == 1:
                    t = n // AH - 1
                    dve.wait_ge(o_full, t + 1)
                    dve.wait_ge(p_ready, AH * (t + 1))
                    astep(dve.reciprocal(att_rec[:, :], att_sum[:, t % 2, :]))
                    if t:
                        filled(dve, ("at", t - 1))
                    dve.tensor_tensor(ao[:, :].rearrange("p (h d) -> p h d", h=AH),
                                      ps[NB][:, :].rearrange("p (h d) -> p h d", h=AH),
                                      att_rec[:, :].unsqueeze(2).to_broadcast([P, AH, AD]), ALU.mult).then_inc(o_copied, 1)
            lstep = serial(dve, ln_step)

            def ln1_finish(t):
                dve.wait_ge(ln_root, t + 1)
                lstep(dve.reciprocal(ln_rstd[:, t % 2, 0:1], ln_rstd[:, t % 2, 0:1]))
                dve.scalar_tensor_tensor(out=ln_rstd[:, t % 2, 1:2], in0=ln_mv[:, t % 2, 0:1], scalar=-1.0,
                                         in1=ln_rstd[:, t % 2, 0:1], op0=ALU.mult, op1=ALU.mult).then_inc(ln_sb, 1)

            def ln1_affine(t):
                dve.wait_ge(ln_norm, t + 1)
                lstep(dve.tensor_tensor(h1all[:, t, :], h1all[:, t, :], lnp[:, 0, :], ALU.mult))
                dve.tensor_tensor(h1all[:, t, :], h1all[:, t, :], lnp[:, 1, :], ALU.add).then_inc(h1_done, 1)

            def router_top(t):
                b = filled(dve, ("rtt", t))
                frees(dve.tensor_tensor(lg[:, t, :], b[:, 0:NE], br[:, :], ALU.add), ("rtt", t))
                copied(dve, ("rtt", t))
                lstep(dve.max(top_v[:, t, :], lg[:, t, :]))
                lstep(dve.max_index(top_i[:, t, :], top_v[:, t, :], lg[:, t, :]))

            dve.wait_ge(xres_in, 64)
            dve.wait_ge(lnp_in, 80)
            for t in range(NT):
                for n in range(2):
                    b = filled(dve, ("mix", t, n))
                    half = h1all[:, t, n * 512:(n + 1) * 512]
                    frees(dve.scalar_tensor_tensor(out=half, in0=half, scalar=ALPHA, in1=b[:, :],
                                                   op0=ALU.mult, op1=ALU.add), ("mix", t, n))
                for n in range(2):
                    copied(dve, ("mix", t, n))
                    lstep(dve.bn_stats(ln_stat[:, t % 2, n, :], h1all[:, t, n * 512:(n + 1) * 512]))
                dve.bn_aggr(ln_mv[:, t % 2, :], ln_stat[:, t % 2, :, :].rearrange("p a b -> p (a b)")).then_inc(ln_var, 1)
                dve.wait_ge(ln_var, t + 1)
                ln1_finish(t)
                ln1_affine(t)
                if t > 1:
                    router_top(t - 2)
            router_top(NT - 2)
            router_top(NT - 1)
            rs = serial(dve, rt_step)
            rs(dve.tensor_copy(idxf[:, :, :], top_i[:, :, 0:4]))
            dve.tensor_tensor(gexp[:, :, :], top_v[:, :, 0:4], top_v[:, :, 0:1].to_broadcast([P, NT, 4]),
                              ALU.subtract).then_inc(rt_diff, 1)
            k_inner = hot[:, :, :, :].rearrange("p t k e -> p t e k")
            iota_tk = iota_e.unsqueeze(1).to_broadcast([P, 4, NE])
            for t in range(NT):
                rs(dve.tensor_tensor(hot[:, t, :, :], iota_tk, idxf[:, t, :].unsqueeze(2).to_broadcast([P, 4, NE]),
                                     ALU.is_equal))
            rs(dve.tensor_reduce(picks[:, :, :], k_inner, AX.X, ALU.add))
            dve.tensor_copy(picks_b[:, :, :], picks[:, :, :]).then_inc(picks_done, 1)
            dve.wait_ge(rt_exp, 1)
            rs(dve.tensor_reduce(gsum[:, 0, :], gexp[:, :, :], AX.X, ALU.add))
            rs(dve.reciprocal(gsum[:, 1, :], gsum[:, 0, :]))
            rs(dve.tensor_tensor(gexp[:, :, :], gexp[:, :, :], gsum[:, 1, :].unsqueeze(2).to_broadcast([P, NT, 4]), ALU.mult))
            for t in range(NT):
                rs(dve.tensor_tensor(hot[:, t, :, :], hot[:, t, :, :], gexp[:, t, :].unsqueeze(2).to_broadcast([P, 4, NE]),
                                     ALU.mult))
            dve.tensor_reduce(gates[:, :, :], k_inner, AX.X, ALU.add).then_inc(gates_done, 1)
            b = filled(dve, ("cnt",))
            rs(dve.tensor_copy(tot[:, :, :].rearrange("p t e -> p (t e)"), b[:, 0:256]))
            rs(dve.memset(base[:, 0, :], 0.0))
            for t in range(1, NT):
                rs(dve.tensor_tensor(base[:, t, :], base[:, t - 1, :], tot[:, t - 1, :], ALU.add))
            count, n_of, ends, first, near, aux = (rt_t[:, k, :] for k in range(6))
            rs(dve.tensor_tensor(count, base[:, NT - 1, :], tot[:, NT - 1, :], ALU.add))
            rs(dve.tensor_scalar(n_of, count, float(CAP), 1.0, ALU.is_gt, ALU.add))
            for k in range(2, S // CAP):
                rs(dve.scalar_tensor_tensor(out=n_of, in0=count, scalar=float(CAP * k), in1=n_of, op0=ALU.is_gt, op1=ALU.add))
            rs(dve.tensor_tensor_scan(ends, onesf[:, 0:NE], n_of, 0.0, ALU.mult, ALU.add))
            rs(dve.tensor_tensor(first, ends, n_of, ALU.subtract))
            rs(dve.tensor_scalar(near, first, float(CAP), None, ALU.mult))
            rs(dve.tensor_tensor(gslot[:, :, :].rearrange("p t e -> p (t e)"), base[:, :, :].rearrange("p t e -> p (t e)"),
                                 b[:, 256:512], ALU.add))
            rs(dve.tensor_tensor(gslot[:, :, :], gslot[:, :, :], near.unsqueeze(1).to_broadcast([P, NT, NE]), ALU.add))
            rs(dve.tensor_scalar(gslot[:, :, :], gslot[:, :, :], 1.0e6, None, ALU.add))
            rs(dve.tensor_tensor(gslot[:, :, :], gslot[:, :, :], picks[:, :, :], ALU.mult))
            frees(dve.tensor_scalar(gslot[:, :, :], gslot[:, :, :], -1.0e6, None, ALU.add), ("cnt",))
            item = consts[:, C_COL:C_COL + 1]
            rs(dve.tensor_scalar(near, ends, item, None, ALU.is_le))
            rs(dve.tensor_reduce(rt_c[:, 2:3], near, AX.X, ALU.add))
            rs(dve.tensor_scalar(rt_c[:, 0:1], rt_c[:, 2:3], float(NE - 1), None, ALU.min))
            rs(dve.tensor_tensor(aux, near, n_of, ALU.mult))
            rs(dve.tensor_reduce(rt_c[:, 3:4], aux, AX.X, ALU.add))
            rs(dve.tensor_scalar(near, iota_e, rt_c[:, 0:1], None, ALU.is_equal))
            rs(dve.tensor_tensor(aux, near, count, ALU.mult))
            rs(dve.tensor_reduce(rt_c[:, 4:5], aux, AX.X, ALU.add))
            rs(dve.tensor_tensor(rt_c[:, 5:6], rt_c[:, 3:4], item, ALU.subtract))
            rs(dve.scalar_tensor_tensor(out=rt_c[:, 6:7], in0=rt_c[:, 5:6], scalar=float(CAP), in1=rt_c[:, 4:5],
                                        op0=ALU.mult, op1=ALU.add))
            rs(dve.tensor_scalar(rt_c[:, 7:8], rt_c[:, 6:7], float(P), None, ALU.is_gt))
            rs(dve.tensor_scalar(rt_c[:, 8:9], ends[:, NE - 1:NE], item, None, ALU.is_gt))
            dve.tensor_tensor(rt_c[:, 1:2], rt_c[:, 7:8], rt_c[:, 8:9], ALU.mult).then_inc(items_done, 1)
            b = filled(dve, ("items",))
            rs(dve.tensor_copy(rt_row[:, 0, :], b[0:1, 0:MAX_ITEMS]))
            frees(dve.tensor_copy(rt_row[:, 1, :], b[0:1, P:P + MAX_ITEMS]), ("items",))
            copied(dve, ("items",))
            rs(dve.tensor_tensor_scan(rt_row[:, 3, :], onesf[0:1, 0:MAX_ITEMS], rt_row[:, 1, :], 0.0, ALU.mult, ALU.add))
            rs(dve.tensor_tensor(rt_row[:, 2, :], rt_row[:, 3, :], rt_row[:, 1, :], ALU.subtract))
            rs(dve.memset(rt_row[:, 3, :], 0.0))
            rs(dve.tensor_copy(rt_row[:, 3, 0:1], ends[0:1, NE - 1:NE]))
            dve.tensor_copy(table[:, :], rt_row[:, :, :].rearrange("p a b -> p (a b)")).then_inc(table_done, 1)
            for t in range(NT):
                if t >= 2:
                    dve.wait_ge(acc_out[t % 2], 16 * (t // 2))
                for n in range(2):
                    b = filled(dve, ("bd", t, n))
                    frees(dve.scalar_tensor_tensor(out=accst[:, t % 2, n * 512:(n + 1) * 512],
                                                   in0=h1all[:, t, n * 512:(n + 1) * 512], scalar=ALPHA, in1=b[:, :],
                                                   op0=ALU.mult, op1=ALU.add), ("bd", t, n))
                    copied(dve, ("bd", t, n))
                dve.sem_inc(acc_half, 1)

            entry = item_table(dve)
            dve.wait_ge(table_done, 1)
            n_items = dve.value_load(table[0:1, 3 * MAX_ITEMS:3 * MAX_ITEMS + 1], min_val=NE, max_val=MAX_ITEMS)

            def mark_slots(e, item, count):
                dve.tensor_scalar(relv[:, :], gslot[:, :, bass.ds(e, 1)].rearrange("p t o -> p (t o)"),
                                  consts[:, bass.ds(item + C_BASE, 1)], None, ALU.subtract).then_inc(rel_done, 1)
                dve.wait_ge(rel_done, count)
                dve.tensor_tensor(slots[:, :, :], consts[:, C_IOTA:C_IOTA + CAP].unsqueeze(1).to_broadcast([P, NT, CAP]),
                                  relv[:, :].unsqueeze(2).to_broadcast([P, NT, CAP]), ALU.is_equal).then_inc(slots_done, 1)

            def find_index(fill, steps, kept):
                dve.wait_ge(tr_full[0], fill)
                dve.tensor_copy(slot_n[:, :, :], ps[TR_BANK[0]][:, 0:8].rearrange("p (b k) -> p b k", b=2)[:, :, 0:3])\
                   .then_inc(tr_free[0], 1)
                dve.wait_ge(tr_free[0], fill)
                dve.scalar_tensor_tensor(out=slot_a[:, 0, :], in0=slot_n[:, :, 1], scalar=float(P), in1=slot_n[:, :, 0],
                                         op0=ALU.mult, op1=ALU.add).then_inc(idx_step, 1)
                dve.tensor_scalar(slot_a[:, 1, :], slot_n[:, :, 2], -4096.0, 4096.0, ALU.mult, ALU.add).then_inc(idx_step, 1)
                dve.wait_ge(idx_step, steps)
                dve.wait_ge(idx_kept, kept)
                dve.tensor_tensor(idx_next[:, :], slot_a[:, 0, :], slot_a[:, 1, :], ALU.add).then_inc(idx_done, 1)

            def take_lo(j, pieces=(0, 1, 2), i=0):
                for g in pieces:
                    dve.wait_ge(hi_done, i * 24 + (4 * j + g + 1))
                    s = slice(2 * g, 2 * g + 2)
                    dve.tensor_tensor(wlo[:, j % 2, s, :], raw[:, (j + 2) % 3, s, :], whi[:, j % 2, s, :].bitcast(f32),
                                      ALU.subtract).then_inc(lo_done, 1)

            def turned_lo(hi_buf, lo_buf, pair, count, width=2):
                n, w = pair % 2, width * P
                dve.wait_ge(tr_hi[n], count)
                s = (slice(None), slice(2 * pair, 2 * pair + 2), slice(0, w))
                dve.tensor_tensor(lo_buf[s], ps[TR_BANK[n]][:, :].rearrange("p (k q) -> p k q", q=2 * P)[:, :, 0:w],
                                  hi_buf[s].bitcast(f32), ALU.subtract).then_inc(tr_free[n], 1)

            def add_biases(quarter, i, n1, blocks, some):
                for b in some:
                    c = n1 if b else i
                    if b:
                        dve.wait_ge(gu_full1, c * 4 + (quarter + 1))
                    else:
                        dve.wait_ge(piece_used, i * 24 + (4 * quarter + 4))
                    dve.wait_ge(bgu_in, i * 16 + 16)
                    dve.wait_ge(hb_done[b], since(c * 4, quarter - 1))
                    n, uses = gu_place(b, quarter, i, n1, blocks)
                    both = gu[:, b, quarter % 2, :]
                    dve.tensor_tensor(both, ps[n][:, :], bgu[:, quarter * SLAB:(quarter + 1) * SLAB], ALU.add)\
                       .then_inc(gu_read[n], 1)
                    dve.wait_ge(gu_read[n], since(uses + 1))
                    dve.tensor_scalar(both[:, 0:256], both[:, 0:256], LIMIT, None, ALU.min).then_inc(clip_g[b], 1)
                    dve.tensor_scalar(both[:, 256:512], both[:, 256:512], LIMIT, -LIMIT, ALU.min, ALU.max)\
                       .then_inc(clip_u[b], 1)

            def item(i, n1, e, ex, blocks):
                for j in range(4):
                    if j == 1:
                        dve.wait_ge(y_done[0], since(i * 2))
                        dve.wait_ge(y_done[1], since(n1 * 2))
                        dve.wait_ge(tokens_in, i + 1)
                        dve.tensor_copy(gcol[:, :], xg[:, :, bass.ds(e + D, 1)].rearrange("p b o -> p (b o)")).then_inc(gate_cp, 1)
                        find_index(fills_before(i, 0) + 1, i * 2 + 4, i + 1)
                    add_biases(j, i, n1, blocks, blocks[:-1])
                    take_lo(j + 2, i=i)
                    add_biases(j, i, n1, blocks, blocks[-1:])
                    if j == 2:
                        turned_lo(hhi, hlo, 0, fill_of(i, "h", 0, 0), len(blocks))
                        turned_lo(hhi, hlo, 1, fill_of(i, "h", 1, 0), len(blocks))
                    if j == 3:
                        turned_lo(hhi, hlo, 2, fill_of(i, "h", 2, 0), len(blocks))
                take_lo(6, (0, 1), i)
                for pair in range(2):
                    turned_lo(xhi, xlo, pair, fill_of(i, "x", pair, 0))
                take_lo(6, (2,), i)
                turned_lo(hhi, hlo, 3, fill_of(i, "h", 3, 0), len(blocks))
                take_lo(7, (0, 1), i)
                turned_lo(xhi, xlo, 2, fill_of(i, "x", 2, 0))
                turned_lo(xhi, xlo, 3, fill_of(i, "x", 3, 0))
                take_lo(7, (2,), i)
                mark_slots(ex, i + 2, i + 3)

            starts(dve, gu_read)
            for n in range(2):
                dve.wait_ge(acc_out[n], 8 * NT)
            dve.wait_ge(h_out, 16 * NT)
            dve.tensor_scalar(relv[:, :], gslot[:, :, 0], 0.0, None, ALU.subtract).then_inc(rel_done, 1)
            dve.wait_ge(rel_done, 1)
            dve.tensor_tensor(slots[:, :, :], consts[:, C_IOTA:C_IOTA + CAP].unsqueeze(1).to_broadcast([P, NT, CAP]),
                              relv[:, :].unsqueeze(2).to_broadcast([P, NT, CAP]), ALU.is_equal).then_inc(slots_done, 1)
            find_index(1, 2, 0)
            take_lo(0)
            take_lo(1)
            mark_slots(entry(0, 1, NE - 1), 1, 2)
            for pair in range(4):
                turned_lo(xhi, xlo, pair, (1, 1, 2, 2)[pair])
            with dve.Fori(0, n_items) as i:
                b1, n1 = entry(1, i, 1), entry(2, i, MAX_ITEMS)
                e, ex = entry(0, i, NE - 1), entry(0, i + 2, NE - 1)
                with dve.If(b1 > 0):
                    item(i, n1, e, ex, (1, 0))
                with dve.If(b1 < 1):
                    item(i, n1, e, ex, (0,))
            fs = serial(dve, f_step)
            dve.wait_ge(lnq_in, 32)
            for t in range(NT):
                dve.wait_ge(fin_in[t // 4], 16)
                for n in range(2):
                    fs(dve.bn_stats(fstat[:, t, n, :], fin[:, t, n * 512:(n + 1) * 512]))
                dve.bn_aggr(fmv[:, t, :], fstat[:, t, :, :].rearrange("p a b -> p (a b)")).then_inc(f_var, 1)
                dve.wait_ge(f_root, t + 1)
                fs(dve.reciprocal(frs[:, 0, t:t + 1], frs[:, 0, t:t + 1]))
                dve.scalar_tensor_tensor(out=frs[:, 1, t:t + 1], in0=fmv[:, t, 0:1], scalar=-1.0,
                                         in1=frs[:, 0, t:t + 1], op0=ALU.mult, op1=ALU.mult).then_inc(f_sb, 1)
                dve.wait_ge(f_norm, t + 1)
                fs(dve.tensor_tensor(fin[:, t, :], fin[:, t, :], lnq[:, 0, :], ALU.mult))
                dve.tensor_tensor(fin[:, t, :], fin[:, t, :], lnq[:, 1, :], ALU.add).then_inc(f_done, 1)

        @block.gpsimd
        def _(pool):
            pool.memset(vaug[:, :, :, MD:MD + 1], 1.0).then_inc(ones_set, 1)
            filled(pool, last_sc)
            pool.memset(uT[:, :, 0:3], 0.0).then_inc(pad_set, 1)
            pool.wait_ge(late_in, 32)
            pool.wait_ge(pad_set, 1)
            pool.wait_ge(score_acc, n_sc)
            cs = serial(pool, conv_step)
            for m in range(4):
                for n in range(2):
                    copied(pool, ("u", m, n))
                if m:
                    pool.wait_ge(conv_done, m)
                tap = ucT[:, m + 1, :] if m < 3 else uT[:, 0, 0:S]
                cs(pool.tensor_scalar(ucT[:, m, :], uT[:, m, 0:S], convw[:, m, 0:1], None, ALU.mult))
                for k in range(1, 4):
                    cs(pool.tensor_scalar(tap, uT[:, m, k:k + S], convw[:, m, k:k + 1], None, ALU.mult))
                    ins = pool.tensor_tensor(ucT[:, m, :], ucT[:, m, :], tap, ALU.add)
                    if k < 3:
                        cs(ins)
                ins.then_inc(conv_done, 1)
            pool.wait_ge(normg_in, 16)
            for t in range(NT):
                copied(pool, ("z", t))
                pool.tensor_tensor(zs[:, t, :, :].rearrange("p h d -> p (h d)"), zs[:, t, :, :].rearrange("p h d -> p (h d)"),
                                   normg[:, :], ALU.mult).then_inc(zgated, 1)
            for c in range(NT - 1):
                copied(pool, ("v", c))
                copied(pool, ("gcol",))
                if c:
                    filled(pool, ("U", c - 1, 1))
                pool.tensor_tensor(mwv[:, :, :], vaug[:, c, :, :], gate_at(3, c).unsqueeze(2).to_broadcast([P, 4, MD + 1]),
                                   ALU.mult).then_inc(wv_done, 1)
                if c:
                    filled(pool, ("X", c, 1))
                    pool.tensor_tensor(mC[:, :, :], mC[:, :, :], gate_at(4, c).unsqueeze(2).to_broadcast([P, 4, MD + 1]),
                                       ALU.mult).then_inc(c_decayed, 1)
            for c in range(NT):
                pool.wait_ge(mnormed, 4 * (c + 1))
                pool.wait_ge(zgated, NT)
                pool.tensor_tensor(zs[:, c, :, :], vaug[:, c, :, 0:MD], zs[:, c, :, :], ALU.mult).then_inc(mout, 1)
            for n in range(2):
                pool.wait_ge(acc_out[n], 8 * NT)
            pool.wait_ge(h_out, 16 * NT)
            pool.wait_ge(gate_out, 16)
            pool.memset(xg[:, :, :], 0.0).then_inc(xg_set, 1)
            pool.wait_ge(xg_set, 1)
            entry = item_table(pool)
            pool.wait_ge(table_done, 1)
            n_items = pool.value_load(table[0:1, 3 * MAX_ITEMS:3 * MAX_ITEMS + 1], min_val=NE, max_val=MAX_ITEMS)

            def fetch(b):
                pool.indirect_dma_start(xg[:, b, :], None, hext, bass.IndirectOffsetOnAxis(idx_next[:, b:b + 1], 0),
                                        bounds_check=S - 1, oob_is_err=False).then_inc(gathered[b], 16)

            def give(b):
                pool.indirect_dma_start(acc, bass.IndirectOffsetOnAxis(idx_cur[:, b:b + 1], 0), ysb[:, b, :], None,
                                        bounds_check=S - 1, oob_is_err=False, compute_op=ALU.add).then_inc(added[b], 16)

            def until(s, value):
                pool.wait_ge(s, value)
                pool.sem_inc(pool_passed, 1)

            def swiglu(quarter, i, n1, blocks):
                for b in blocks:
                    c = (n1 if b else i) * 4 + quarter
                    both = gu[:, b, quarter % 2, :]
                    g, u, h = both[:, 0:256], both[:, 256:512], hb[:, b, quarter * 256:(quarter + 1) * 256]
                    until(clip_u[b], c + 1)
                    until(clip_g[b], c + 1)
                    pool.tensor_scalar(u, u, 1.0, 1.0, ALU.add, ALU.mult).then_inc(up_done[b], 1)
                    until(up_done[b], c * 2 + 1)
                    pool.tensor_tensor(u, u, g, ALU.mult).then_inc(up_done[b], 1)
                    until(up_done[b], c * 2 + 2)
                    until(sig_done[b], c + 1)
                    pool.tensor_tensor(h, h, u, ALU.mult).then_inc(hb_done[b], 1)

            def take_last_lo(j, i=0):
                until(hi_done, i * 24 + (4 * j + 4))
                pool.tensor_tensor(wlo[:, j % 2, 6:8, :], raw[:, (j + 2) % 3, 6:8, :], whi[:, j % 2, 6:8, :].bitcast(f32),
                                   ALU.subtract).then_inc(lo3_done, 1)

            def item(i, n1, n1x, b1x, blocks):
                for j in range(4):
                    if j == 1:
                        until(idx_done, i + 2)
                        until(gate_cp, i + 1)
                        for n in range(2):
                            until(tr_full[n], fills_before(i, n))
                        fetch(0)
                        with pool.If(b1x > 0):
                            fetch(1)
                    if j == 2:
                        with pool.If(i > 0):
                            until(added[0], i * 16)
                        with pool.If(n1 > 0):
                            until(added[1], n1 * 16)
                        pool.tensor_copy(idx_cur[:, :], idx_mid[:, :]).then_inc(sum_kept, 1)
                        until(sum_kept, i + 1)
                        pool.tensor_copy(idx_mid[:, :], idx_next[:, :]).then_inc(idx_kept, 1)
                    swiglu(j, i, n1, blocks[:-1])
                    if j == 3:
                        until(gathered[0], i * 16 + 32)
                        with pool.If(b1x > 0):
                            until(gathered[1], n1x * 16 + 16)
                        pool.sem_inc(tokens_in, 1)
                    if len(blocks) == 2:
                        take_last_lo(j + 2, i)
                    swiglu(j, i, n1, blocks[-1:])
                    if len(blocks) == 1:
                        take_last_lo(j + 2, i)
                take_last_lo(6, i)
                take_last_lo(7, i)
                for b in blocks:
                    until(y_done[b], since((n1 if b else i) * 2 + 2))
                    give(b)
            starts(pool, hb_done)
            take_last_lo(0)
            take_last_lo(1)
            pool.wait_ge(idx_done, 1)
            fetch(0)
            b1_0 = entry(1, 0, 1)
            with pool.If(b1_0 > 0):
                fetch(1)
            pool.wait_ge(gathered[0], 16)
            with pool.If(b1_0 > 0):
                pool.wait_ge(gathered[1], 16)
            pool.sem_inc(tokens_in, 1)
            pool.tensor_copy(idx_mid[:, :], idx_next[:, :]).then_inc(idx_kept, 1)
            with pool.Fori(0, n_items) as i:
                b1, n1 = entry(1, i, 1), entry(2, i, MAX_ITEMS)
                b1x, n1x = entry(1, i + 1, 1), entry(2, i + 1, MAX_ITEMS)
                with pool.If(b1 > 0):
                    item(i, n1, n1x, b1x, (1, 0))
                with pool.If(b1 < 1):
                    item(i, n1, n1x, b1x, (0,))
            until(added[0], n_items * 16)
            n1 = entry(2, n_items, MAX_ITEMS)
            with pool.If(n1 > 0):
                until(added[1], n1 * 16)
            pool.sem_inc(all_added, 1)


def constants():
    import numpy as np
    c = np.zeros((P, C_END), np.float32)
    p = np.arange(P)[:, None]
    c[:, C_ID:C_ID + P] = np.eye(P)
    c[:, C_MASK:C_MASK + P] = np.where(p > np.arange(P)[None], -1e30, 0.0)
    c[:, C_DIST:C_DIST + S] = np.abs(p + (S - P) - np.arange(S)[None])
    c[:, C_IOTA:C_IOTA + CAP] = np.arange(CAP)[None]
    for m in range(4):
        for par in range(2):
            c[par * 64:par * 64 + 64, C_QS + m] = 2.0 ** (2 * m + par + 1) / 8.0
    c[:, C_BASE:C_BASE + MAX_ITEMS + 1] = CAP * np.arange(MAX_ITEMS + 1)[None]
    c[:, C_COL] = np.arange(P)
    c[:, C_COL + 1] = EPS
    c[:, C_ONE:C_ONE + P] = 1.0
    b = np.zeros((P, 2 * P + 24), np.float32)
    b[:, 0:P] = 1.0
    b[:, P:2 * P] = p < np.arange(P)[None]
    for t in range(NT):
        b[:, 2 * P + 3 * t] = np.arange(P)
        b[:, 2 * P + 3 * t + 1] = t
        b[:, 2 * P + 3 * t + 2] = 1.0
    return c, b.astype(mybir.dt.np(mybir.dt.bfloat16))


def kernel(**inputs):
    import numpy as np
    import concourse.bacc as bacc
    from concourse.bass_utils import run_bass_kernel_spmd

    v = {k: np.asarray(x) for k, x in inputs.items()}

    def slab(w):
        return np.ascontiguousarray(w.reshape(KT, P, -1).transpose(1, 0, 2))

    w = v["w_in"][0]
    sizes = (512, 128, 512, 64, 8, 512, 512, 512, 4, 4)
    ends = np.cumsum(sizes)
    q_a, ckv, q_i, k_i, w_i, u, vv, z, gi, gf = (w[:, e - s:e] for s, e in zip(sizes, ends))
    consts, cb = constants()
    arrays = {
        "xT": slab(np.ascontiguousarray(v["x"][0].T)),
        "x": np.ascontiguousarray(v["x"][0].reshape(NT, P, D).transpose(1, 0, 2)),
        "w_qi": slab(q_i),
        "w_ks": slab(np.concatenate([k_i, k_i, ckv, w_i, gi, gf], axis=1)),
        "w_qa": slab(q_a), "w_u": slab(u), "w_v": slab(vv), "w_z": slab(z),
        "w_out": np.stack([slab(v["w_out"][0][:, n * 512:(n + 1) * 512]) for n in range(2)]),
        "kv_norm_g": np.ascontiguousarray(v["kv_norm_g"].reshape(P, 1)),
        "w_ukv": np.ascontiguousarray(np.stack([v["w_uk"][0].transpose(1, 0, 2).reshape(P, 512),
                                                v["w_uv"][0].transpose(1, 0, 2).reshape(P, 512)], axis=1)),
        "conv": np.ascontiguousarray(np.concatenate([v["m_conv_w"][0], v["m_conv_b"]], axis=0)
                                     .reshape(5, 4, P).transpose(2, 1, 0)),
        "w_m": np.ascontiguousarray(np.stack([v["w_mq"][0], v["w_mk"][0]]).transpose(2, 0, 1, 3)),
        "b_if": np.concatenate([v["b_i"][0], v["b_f"][0]]),
        "m_norm_g": v["m_norm_g"][0],
        "ln1_g": v["ln1_g"][0], "ln1_b": v["ln1_b"][0], "ln2_g": v["ln2_g"][0], "ln2_b": v["ln2_b"][0],
        "w_router": slab(v["w_router"][0]), "b_router": v["b_router"][0],
        "w_gu": np.ascontiguousarray(v["w_gu"][0].reshape(NE, KT, P, 2, 4, 256).transpose(0, 4, 2, 1, 3, 5)
                                     .reshape(4 * NE, P, KT, SLAB)),
        "w_dn": np.ascontiguousarray(v["w_down"][0].reshape(NE, 2, 4, P, D).transpose(0, 1, 3, 2, 4)
                                     .reshape(2 * NE, P, KT, SLAB)),
        "b_gu": np.ascontiguousarray(v["b_gu"][0].reshape(NE, 2, 4, 256).transpose(0, 2, 1, 3).reshape(NE, 2 * D)),
        "b_down": v["b_down"][0],
        "consts": consts, "cb": cb,
    }
    nc = bacc.Bacc("TRN2", target_bir_lowering=False, num_devices=1)
    aps = {k: nc.dram_tensor("in_" + k, x.shape, mybir.dt.from_np(x.dtype), kind="ExternalInput").ap()
           for k, x in arrays.items()}
    out = nc.dram_tensor("out", (1, S, D), mybir.dt.float32, kind="ExternalOutput").ap()
    layer_kernel(nc, aps, out)
    got = run_bass_kernel_spmd(nc, [{"in_" + k: x for k, x in arrays.items()}], core_ids=[0])
    return got.results[0]["out"]
```
